# Optimizing a Trainium2 kernel written in Bass

```python
import math
import jax, jax.numpy as jnp
from jax import lax
import numpy as np

D_MODEL = 1024
BATCH = 1
SEQ = 1024
DEPTH = 2

GRID_W = 64
CTX_LEN = 256
HEAD_DIM = 64
BLOCK = 128
WINDOW = 128
ATTN_SCALE = HEAD_DIM ** -0.5
ROPE_THETA = 10000.0
AXIS_FREQS = HEAD_DIM // 4
A_HEADS = 4
A_KV_HEADS = 2
B_HEADS = 4
B_KV_HEADS = 2
C_HEADS = 8
C_HEAD_DIM = 64
C_INNER = C_HEADS * C_HEAD_DIM
C_GROUPS = 2
C_STATE = 128
C_CONV = 5
C_CHUNK = 128
C_CONV_CH = C_INNER + 2 * C_GROUPS * C_STATE
MIX_WIDTH = (A_HEADS + B_HEADS) * HEAD_DIM + C_INNER
PROJ_SIZES = (A_HEADS * HEAD_DIM, A_KV_HEADS * HEAD_DIM, A_KV_HEADS * HEAD_DIM,
              B_HEADS * HEAD_DIM, B_KV_HEADS * HEAD_DIM, B_KV_HEADS * HEAD_DIM,
              C_INNER, C_CONV_CH, 2 * C_HEADS)
IN_COLS = sum(PROJ_SIZES)
D_FF = -(-8 * D_MODEL // (3 * 256)) * 256
DEEPNORM_ALPHA = (2 * DEPTH) ** 0.25
DEEPNORM_BETA = (8 * DEPTH) ** -0.25
LN_EPS = 1e-5
RMS_EPS = 1e-6
F32 = jnp.float32

kernel_name = 'hybrid_hymba_dit_prefix_block'

def layer_norm(u, g, b):
    uf = u.astype(F32)
    mu = jnp.mean(uf, -1, keepdims=True)
    var = jnp.mean(jnp.square(uf - mu), -1, keepdims=True)
    return ((uf - mu) * lax.rsqrt(var + LN_EPS) * g + b).astype(u.dtype)

def rms_norm(u, g):
    uf = u.astype(F32)
    return (uf * lax.rsqrt(jnp.mean(uf * uf, -1, keepdims=True) + RMS_EPS) * g).astype(u.dtype)

def axial_rope_tables(n):
    rows = n // GRID_W
    row = jnp.repeat(jnp.arange(rows), GRID_W)
    col = jnp.tile(jnp.arange(GRID_W), rows)
    inv = ROPE_THETA ** (-jnp.arange(AXIS_FREQS, dtype=F32) / AXIS_FREQS)
    ang = jnp.stack([row, col], -1).astype(F32)[..., None] * inv
    return jnp.cos(ang), jnp.sin(ang)

def apply_axial_rope(u, cos, sin):
    bsz, n, nh, hd = u.shape
    ur = u.astype(F32).reshape(bsz, n, nh, 2, 2, AXIS_FREQS)
    u1, u2 = ur[..., 0, :], ur[..., 1, :]
    cs, sn = cos[None, :, None], sin[None, :, None]
    out = jnp.stack([u1 * cs - u2 * sn, u1 * sn + u2 * cs], axis=-2)
    return out.reshape(bsz, n, nh, hd).astype(u.dtype)

def split_projection(p):
    offsets = []
    acc = 0
    for s in PROJ_SIZES[:-1]:
        acc += s
        offsets.append(acc)
    return jnp.split(p, offsets, axis=-1)

def to_heads(t):
    return t.reshape(t.shape[0], t.shape[1], -1, HEAD_DIM)

def window_sink_attention(q, k, v, kc, vc, sink):
    bsz, n, nh, hd = q.shape
    nkv = k.shape[2]
    grp = nh // nkv
    nb = n // BLOCK
    lc = kc.shape[1]

    def windows(t):
        tp = jnp.pad(t, ((0, 0), (BLOCK, BLOCK), (0, 0), (0, 0))).reshape(bsz, nb + 2, BLOCK, nkv, hd)
        return jnp.concatenate([tp[:, :-2], tp[:, 1:-1], tp[:, 2:]], axis=2)

    kw, vw = windows(k), windows(v)
    qb = (q * ATTN_SCALE).reshape(bsz, nb, BLOCK, nkv, grp, hd)
    s_loc = jnp.einsum('bnqkgd,bnskd->bnkgqs', qb, kw).astype(F32)
    s_ctx = jnp.einsum('bnqkgd,bckd->bnkgqc', qb, kc).astype(F32)
    qi = jnp.arange(BLOCK)[:, None]
    si = jnp.arange(3 * BLOCK)[None, :]
    kpos = (jnp.arange(nb) * BLOCK)[:, None, None] - BLOCK + si[None]
    mask = (jnp.abs(si - BLOCK - qi) <= WINDOW)[None] & (kpos >= 0) & (kpos < n)
    s_loc = jnp.where(mask[None, :, None, None], s_loc, -jnp.inf)
    s_sink = jnp.broadcast_to(sink.astype(F32).reshape(nkv, grp)[:, :, None, None], (bsz, nb, nkv, grp, BLOCK, 1))
    p = jax.nn.softmax(jnp.concatenate([s_loc, s_ctx, s_sink], -1), -1).astype(v.dtype)
    w = 3 * BLOCK
    out = (jnp.einsum('bnkgqs,bnskd->bnqkgd', p[..., :w], vw)
           + jnp.einsum('bnkgqc,bckd->bnqkgd', p[..., w:w + lc], vc))
    return out.reshape(bsz, n, nh * hd)

def global_block_attention(q, k, v, kc, vc):
    bsz, n, nh, hd = q.shape
    nkv = k.shape[2]
    grp = nh // nkv
    k_all = jnp.concatenate([k, kc], axis=1)
    v_all = jnp.concatenate([v, vc], axis=1)
    qb = jnp.moveaxis((q * ATTN_SCALE).reshape(bsz, n // BLOCK, BLOCK, nkv, grp, hd), 1, 0)

    def one_block(qblk):
        s = jnp.einsum('bqkgd,bskd->bkgqs', qblk, k_all).astype(F32)
        p = jax.nn.softmax(s, -1).astype(v_all.dtype)
        return jnp.einsum('bkgqs,bskd->bqkgd', p, v_all)

    out = lax.map(one_block, qb)
    return jnp.moveaxis(out, 0, 1).reshape(bsz, n, nh * hd)

def ctx_attention(q, k, v, sink):
    bsz, lc, nh, hd = q.shape
    nkv = k.shape[2]
    grp = nh // nkv
    s = jnp.einsum('bqkgd,bskd->bkgqs', (q * ATTN_SCALE).reshape(bsz, lc, nkv, grp, hd), k).astype(F32)
    if sink is not None:
        s_sink = jnp.broadcast_to(sink.astype(F32).reshape(nkv, grp)[:, :, None, None], (bsz, nkv, grp, lc, 1))
        s = jnp.concatenate([s, s_sink], -1)
    p = jax.nn.softmax(s, -1)[..., :lc].astype(v.dtype)
    return jnp.einsum('bkgqs,bskd->bqkgd', p, v).reshape(bsz, lc, nh * hd)

def centred_dwconv(u, w, b):
    out = lax.conv_general_dilated(u, w[:, None, :].astype(u.dtype), window_strides=(1,),
                                   padding=((C_CONV // 2, C_CONV // 2),),
                                   dimension_numbers=('NWC', 'WIO', 'NWC'),
                                   feature_group_count=u.shape[-1])
    return out + b

def ssd_inputs(xbc, dt_raw, conv_w, conv_b, dt_bias):
    bsz, n, _ = xbc.shape
    u = jax.nn.silu(centred_dwconv(xbc, conv_w, conv_b))
    xs, bm, cm = jnp.split(u, [C_INNER, C_INNER + C_GROUPS * C_STATE], axis=-1)
    xs = xs.reshape(bsz, n, C_HEADS, C_HEAD_DIM)
    bm = bm.reshape(bsz, n, C_GROUPS, C_STATE)
    cm = cm.reshape(bsz, n, C_GROUPS, C_STATE)
    dt = jax.nn.softplus(dt_raw.astype(F32).reshape(bsz, n, 2, C_HEADS) + dt_bias.astype(F32))
    return xs, bm, cm, dt[:, :, 0], dt[:, :, 1]

def ssd_scan(xs, dt, a, bm, cm, h0, with_y):
    bsz, n, nh, hp = xs.shape
    nc = n // C_CHUNK
    rep = nh // C_GROUPS
    xd = (xs.astype(F32) * dt[..., None]).reshape(bsz, nc, C_CHUNK, nh, hp)
    bh = jnp.repeat(bm.astype(F32), rep, axis=2).reshape(bsz, nc, C_CHUNK, nh, C_STATE)
    acum = jnp.cumsum((dt * a).reshape(bsz, nc, C_CHUNK, nh), axis=2)
    decay_to_end = jnp.exp(acum[:, :, -1:] - acum)
    chunk_states = jnp.einsum('bclhn,bclhp->bchpn', bh * decay_to_end[..., None], xd)
    chunk_decay = jnp.exp(acum[:, :, -1])

    def step(state, inp):
        st, dec = inp
        return state * dec[:, :, None, None] + st, state

    h_final, h_start = lax.scan(step, h0, (jnp.moveaxis(chunk_states, 1, 0), jnp.moveaxis(chunk_decay, 1, 0)))
    if not with_y:
        return None, h_final
    ch = jnp.repeat(cm.astype(F32), rep, axis=2).reshape(bsz, nc, C_CHUNK, nh, C_STATE)
    h_start = jnp.moveaxis(h_start, 0, 1)
    li = jnp.arange(C_CHUNK)
    causal = li[:, None] >= li[None, :]
    seg = acum[:, :, :, None, :] - acum[:, :, None, :, :]
    lmat = jnp.exp(jnp.where(causal[None, None, :, :, None], seg, -jnp.inf))
    scores = jnp.einsum('bclhn,bcshn->bclsh', ch, bh) * lmat
    y_diag = jnp.einsum('bclsh,bcshp->bclhp', scores, xd)
    y_off = jnp.einsum('bclhn,bchpn->bclhp', ch, h_start) * jnp.exp(acum)[..., None]
    return (y_diag + y_off).reshape(bsz, n, nh, hp), h_final

def bidir_ssd(xs, bm, cm, dt_f, dt_b, a_f, a_b, h0_f, h0_b, with_y):
    rev = lambda t: jnp.flip(t, axis=1)
    y_f, hf = ssd_scan(xs, dt_f, a_f, bm, cm, h0_f, with_y)
    y_b, hb = ssd_scan(rev(xs), rev(dt_b), a_b, rev(bm), rev(cm), h0_b, with_y)
    y = y_f + rev(y_b) if with_y else None
    return y, hf, hb

def ssd_output(y, xs, z, d_skip, gnorm_w):
    bsz, n = z.shape[:2]
    y = y + xs.astype(F32) * d_skip.astype(F32)[:, None]
    g = (y.reshape(bsz, n, C_INNER) * jax.nn.silu(z.astype(F32))).reshape(bsz, n, C_GROUPS, C_INNER // C_GROUPS)
    g = g * lax.rsqrt(jnp.mean(g * g, -1, keepdims=True) + RMS_EPS)
    return (g.reshape(bsz, n, C_INNER) * gnorm_w).astype(z.dtype)

def hybrid_mixer(h, hc, cos, sin, w_in, sink, q_gain, k_gain, conv_w, conv_b, a_log, dt_bias, d_skip,
                 gnorm_w, w_out, with_ctx_out):
    bsz = h.shape[0]
    aq, ak, av, bq, bk, bv, z, xbc, dt = split_projection(h @ w_in)
    caq, cak, cav, cbq, cbk, cbv, cz, cxbc, cdt = split_projection(hc @ w_in)
    cak, cav = to_heads(cak), to_heads(cav)
    out_a = window_sink_attention(apply_axial_rope(to_heads(aq), cos, sin), apply_axial_rope(to_heads(ak), cos, sin),
                                  to_heads(av), cak, cav, sink)
    cbk, cbv = rms_norm(to_heads(cbk), k_gain), to_heads(cbv)
    out_b = global_block_attention(apply_axial_rope(rms_norm(to_heads(bq), q_gain), cos, sin),
                                   apply_axial_rope(rms_norm(to_heads(bk), k_gain), cos, sin),
                                   to_heads(bv), cbk, cbv)
    a_f = -jnp.exp(a_log[0].astype(F32))
    a_b = -jnp.exp(a_log[1].astype(F32))
    cxs, cbm, ccm, cdt_f, cdt_b = ssd_inputs(cxbc, cdt, conv_w, conv_b, dt_bias)
    zeros = jnp.zeros((bsz, C_HEADS, C_HEAD_DIM, C_STATE), F32)
    cy, st_f, st_b = bidir_ssd(cxs, cbm, ccm, cdt_f, cdt_b, a_f, a_b, zeros, zeros, with_ctx_out)
    xs, bm, cm, dt_f, dt_b = ssd_inputs(xbc, dt, conv_w, conv_b, dt_bias)
    y_c, _, _ = bidir_ssd(xs, bm, cm, dt_f, dt_b, a_f, a_b, st_f, st_b, True)
    out_c = ssd_output(y_c, xs, z, d_skip, gnorm_w)
    y = jnp.concatenate([out_a, out_b, out_c], -1) @ w_out
    if not with_ctx_out:
        return y, None
    ca = ctx_attention(to_heads(caq), cak, cav, sink)
    cb = ctx_attention(rms_norm(to_heads(cbq), q_gain), cbk, cbv, None)
    cc = ssd_output(cy, cxs, cz, d_skip, gnorm_w)
    yc = jnp.concatenate([ca, cb, cc], -1) @ w_out
    return y, yc

def swiglu(h, w_gu, w_down):
    gate, up = jnp.split(h @ w_gu, 2, axis=-1)
    return (jax.nn.silu(gate) * up) @ w_down

def setup_inputs(seed: int = 0) -> dict:
    key = jax.random.key(seed)
    ks = jax.random.split(key, 23)
    nrm = lambda k, shape, scale: jax.random.normal(k, shape, F32) * scale
    dt0 = jnp.exp(jax.random.uniform(ks[13], (DEPTH, 2, C_HEADS), F32, math.log(1e-3), math.log(1e-1)))
    return {
        'x': nrm(ks[0], (BATCH, SEQ, D_MODEL), 1.0),
        'c': nrm(ks[1], (BATCH, D_MODEL), 1.0),
        'ctx': nrm(ks[2], (BATCH, CTX_LEN, D_MODEL), 1.0),
        'c_ctx': nrm(ks[3], (D_MODEL,), 1.0),
        'w_ada': nrm(ks[4], (DEPTH, D_MODEL, 6 * D_MODEL), 0.5 * D_MODEL ** -0.5),
        'b_ada': nrm(ks[5], (DEPTH, 6 * D_MODEL), 0.01),
        'w_in': nrm(ks[6], (DEPTH, D_MODEL, IN_COLS), D_MODEL ** -0.5),
        'sink': nrm(ks[7], (DEPTH, A_HEADS), 0.5),
        'q_gain': 1.0 + nrm(ks[8], (DEPTH, HEAD_DIM), 0.02),
        'k_gain': 1.0 + nrm(ks[9], (DEPTH, HEAD_DIM), 0.02),
        'conv_w': nrm(ks[10], (DEPTH, C_CONV, C_CONV_CH), C_CONV ** -0.5),
        'conv_b': nrm(ks[11], (DEPTH, C_CONV_CH), 0.01),
        'a_log': jnp.log(jax.random.uniform(ks[12], (DEPTH, 2, C_HEADS), F32, 1.0, 16.0)),
        'dt_bias': dt0 + jnp.log(-jnp.expm1(-dt0)),
        'd_skip': 1.0 + nrm(ks[14], (DEPTH, C_HEADS), 0.02),
        'gnorm_w': 1.0 + nrm(ks[15], (DEPTH, C_INNER), 0.02),
        'w_out': nrm(ks[16], (DEPTH, MIX_WIDTH, D_MODEL), DEEPNORM_BETA * MIX_WIDTH ** -0.5),
        'ln1_g': 1.0 + nrm(ks[17], (DEPTH, D_MODEL), 0.02),
        'ln1_b': nrm(ks[18], (DEPTH, D_MODEL), 0.01),
        'ln2_g': 1.0 + nrm(ks[19], (DEPTH, D_MODEL), 0.02),
        'ln2_b': nrm(ks[20], (DEPTH, D_MODEL), 0.01),
        'w_gu': nrm(ks[21], (DEPTH, D_MODEL, 2 * D_FF), D_MODEL ** -0.5),
        'w_down': nrm(ks[22], (DEPTH, D_FF, D_MODEL), DEEPNORM_BETA * D_FF ** -0.5),
    }

def reference(x, c, ctx, c_ctx, w_ada, b_ada, w_in, sink, q_gain, k_gain, conv_w, conv_b, a_log, dt_bias,
              d_skip, gnorm_w, w_out, ln1_g, ln1_b, ln2_g, ln2_b, w_gu, w_down):
    cos, sin = axial_rope_tables(x.shape[1])
    for l in range(DEPTH):
        last = l == DEPTH - 1
        mod = jax.nn.silu(c) @ w_ada[l] + b_ada[l]
        mod_c = jax.nn.silu(c_ctx) @ w_ada[l] + b_ada[l]
        sh1, sc1, g1, sh2, sc2, g2 = jnp.split(mod[:, None, :], 6, axis=-1)
        csh1, csc1, cg1, csh2, csc2, cg2 = jnp.split(mod_c, 6)
        y, yc = hybrid_mixer(x * (1 + sc1) + sh1, ctx * (1 + csc1) + csh1, cos, sin, w_in[l], sink[l],
                             q_gain[l], k_gain[l], conv_w[l], conv_b[l], a_log[l], dt_bias[l], d_skip[l],
                             gnorm_w[l], w_out[l], not last)
        x = layer_norm(DEEPNORM_ALPHA * x + g1 * y, ln1_g[l], ln1_b[l])
        x = layer_norm(DEEPNORM_ALPHA * x + g2 * swiglu(x * (1 + sc2) + sh2, w_gu[l], w_down[l]), ln2_g[l], ln2_b[l])
        if not last:
            ctx = layer_norm(DEEPNORM_ALPHA * ctx + cg1 * yc, ln1_g[l], ln1_b[l])
            ctx = layer_norm(DEEPNORM_ALPHA * ctx + cg2 * swiglu(ctx * (1 + csc2) + csh2, w_gu[l], w_down[l]),
                             ln2_g[l], ln2_b[l])
    return x


_drawn_inputs = setup_inputs


def setup_inputs(seed=0):
    import zlib

    import numpy as np

    out = dict(_drawn_inputs(seed))
    spreads = {}
    factors = {'ctx': 8.0,
     'c_ctx': 4.588,
     'b_ada': 8.0,
     'sink': 64.0,
     'q_gain': 8.0,
     'k_gain': 8.0,
     'conv_b': 8.0,
     'd_skip': 35.859,
     'gnorm_w': 30.076,
     'ln1_b': 4.07,
     'ln2_b': 4.028}
    for name, (base, spread) in spreads.items():
        noise = np.random.default_rng([zlib.crc32(name.encode()), seed]).standard_normal(out[name].shape)
        drawn = base * np.exp(spread * noise) if base else spread * noise
        out[name] = __import__('jax').numpy.asarray(drawn.astype(out[name].dtype))
    for name, factor in factors.items():
        out[name] = (out[name] * factor).astype(out[name].dtype)
    return out
```

```python
from contextlib import ExitStack

import numpy as np

import concourse.bass as bass
from concourse import mybir

ALU = mybir.AluOpType
ACT = mybir.ActivationFunctionType
AX = mybir.AxisListType
F32 = mybir.dt.float32
F32R = mybir.dt.float32r

P = 128
D = 1024
SEQ = 1024
CTX = 256
TOK = SEQ + CTX
DEPTH = 2
GRID_W = 64
HD = 64
HEADS = 4
CH = 8
GROUPS = 2
CONV = 5
D_FF = 2816
KT = D // P
TT = TOK // P
LT = SEQ // P
FT = D_FF // P
SCALE = float(HD) ** -0.5
ALPHA = float((2 * DEPTH) ** 0.25)
LN_EPS = 1e-5
RMS_EPS = 1e-6
NEG = -1.0e30

CHUNKS = ((0, 512), (512, 512), (SEQ, CTX))
ORDER = (2, 0, 1)

IDENT, UPTO, FROM, AFTER, BEFORE, ONES, MEAN, BLOCK64, ROT, MASKS = (P * j for j in range(10))
N_CONST = MASKS + 3 * 3 * P

LN1G, LN1B, LN2G, LN2B = 0, 8, 16, 24
BADA = 32
CONVW = BADA + 48
CONVB = CONVW + 8 * CONV
QGAIN = CONVB + 8
KGAIN = QGAIN + 1
SINK = KGAIN + 1
DTB = SINK + HEADS
ALOG = DTB + 2 * CH
DSKIP = ALOG + 2 * CH
GNORM = DSKIP + CH
N_PRM = GNORM + 512

SH1, SC1, G1, SH2, SC2, G2 = (KT * j for j in range(6))


def const_table():
    t = np.zeros((P, N_CONST), np.float32)
    r, c = np.arange(P)[:, None], np.arange(P)[None, :]
    t[:, IDENT:IDENT + P] = r == c
    t[:, UPTO:UPTO + P] = r <= c
    t[:, FROM:FROM + P] = r >= c
    t[:, AFTER:AFTER + P] = r > c
    t[:, BEFORE:BEFORE + P] = r < c
    t[:, ONES:ONES + P] = 1.0
    t[:, MEAN:MEAN + P] = 1.0 / D
    t[:, BLOCK64:BLOCK64 + P] = (r // HD == c // HD) / float(HD)
    quarter = HD // 4
    first, second = (r // quarter) % 2 == 0, (r // quarter) % 2 == 1
    t[:, ROT:ROT + P] = 1.0 * (first & (c == r + quarter)) - 1.0 * (second & (c == r - quarter))
    left = np.where(c >= r, 0.0, NEG)
    right = np.where(c <= r, 0.0, NEG)
    free, shut = np.zeros((P, P)), np.full((P, P), NEG)
    for v, parts in enumerate(((shut, free, right), (left, free, right), (left, free, shut))):
        t[:, MASKS + 3 * P * v:MASKS + 3 * P * (v + 1)] = np.concatenate(parts, 1)
    return t


def rope_table():
    n = np.arange(SEQ)
    freqs = HD // 4
    inv = np.float32(10000.0) ** (-np.arange(freqs, dtype=np.float32) / np.float32(freqs))
    ang = np.stack([n // GRID_W, n % GRID_W], -1).astype(np.float32)[..., None] * inv
    ang = np.broadcast_to(ang.transpose(1, 2, 0)[None, :, None], (2, 2, 2, freqs, SEQ)).reshape(P, SEQ)
    return np.stack([np.cos(ang), np.sin(ang)], 1).astype(np.float32)


class Plan:

    def __init__(self, nc, ctx, arrays):
        self.nc, self.ctx, self.a = nc, ctx, arrays
        self.stage_sems = []
        self.base = 16512
        self.top = self.base + 14 * 1024
        at = self.at
        self.const = at("const", [P, N_CONST], F32, low=0)
        self.prm = at("prm", [P, N_PRM], F32, low=9216)
        self.mod = at("mod", [P, 48, 2], F32, low=12032)
        self.dtr = at("dtr", [P, TT, 2 * CH], F32, low=12544)
        self.csil = at("csil", [P, KT, 2], F32, low=13184)
        self.cin = at("cin", [P, KT, 2], F32, low=13248)
        self.small = at("small", [P, 32], F32, low=13312)
        self.ssq = at("ssq", [P, TT, GROUPS], F32, low=13440)
        self.hi = at("h_hi", [P, KT, TOK], F32R, kb=0)
        self.lo = at("h_lo", [P, KT, TOK], F32R, kb=40)
        self.x = at("x_res", [P, KT, TOK], F32, kb=80)
        self.qk = at("qk", [P, 6, TOK], F32, kb=80)
        self.v = at("v_tok", [P, TT, 256], F32, kb=110)
        self.mixab = at("mix_ab", [P, TT, 512], F32, kb=120)
        self.mixc = at("mix_c", [P, TT, 512], F32, kb=150)
        self.ps = ctx.enter_context(nc.psum_tensor("ps", [P, 8 * 512], F32))
        self.x_dram = nc.dram_tensor("x_spill", [P, KT, TOK], F32, kind="Internal").ap()
        self.z_dram = nc.dram_tensor("z_spill", [P, TT, 512], F32, kind="Internal").ap()

    def at(self, name, shape, dtype, kb=None, low=None):
        off = self.base + low if kb is None else self.top + int(kb * 1024)
        return self.nc.alloc_sbuf_tensor_at(name, shape, dtype, offset=off)

    def sem(self, name):
        self.stage_sems.append(self.nc.alloc_semaphore(name))
        return self.stage_sems[-1]

    def end_stage(self):
        self.nc.clear_and_free_semaphores(self.stage_sems)
        self.nc.all_engine_barrier()
        self.stage_sems = []

    def c(self, col, n=P):
        return self.const[:, col:col + n]

    def bank(self, b, n=512):
        return self.ps[:, 512 * b:512 * b + n]


def raw(t):
    return t.bitcast(F32)


def three_pass(pe, out, w_hi, w_lo, h_hi, h_lo, first, last):
    pe.matmul(out, w_hi, h_hi, start=first, stop=False)
    pe.matmul(out, w_hi, h_lo, start=False, stop=False)
    return pe.matmul(out, w_lo, h_hi, start=False, stop=last)


class At:

    def __init__(self, n, par, kind, i, j, half, m2):
        self.n, self.par, self.kind, self.i, self.j, self.half, self.m2 = n, par, kind, i, j, half, m2

    def number(self, c):
        return self.m2 if c == 2 else self.n


def over(eng, segments, chunks_of, body):
    n0 = m0 = 0
    for count, kinds in segments:
        with2 = [int(2 in chunks_of(k)) for k in kinds]

        def run(i):
            for j, k in enumerate(kinds):
                body(At(i * len(kinds) + (n0 + j), (n0 + j) % 2, k, i, j,
                        i * (len(kinds) // 2) + (n0 + j) // 2, i * sum(with2) + (m0 + sum(with2[:j]))))
        if count > 1:
            with eng.Fori(0, count) as i:
                run(i)
        else:
            run(0)
        n0 += count * len(kinds)
        m0 += count * sum(with2)



def load_inputs(pl):
    nc, a = pl.nc, pl.a
    loaded = pl.sem("start_loaded")
    with nc.Block() as block:
        @block.sync
        def _(sp):
            sp.dma_start(pl.const[:, :], a["consts"]).then_inc(loaded, 16)
            sp.dma_start(pl.cin[:, :, :], a["cT"]).then_inc(loaded, 16)
            sp.dma_start(pl.x[:, :, :], a["xT"]).then_inc(loaded, 16)
            sp.wait_ge(loaded, 48)
    with nc.Block() as block:
        @block.vector
        def _(dve):
            dve.memset(pl.small[:, 0:1], RMS_EPS)
            dve.memset(pl.small[:, 1:2], LN_EPS)
            dve.memset(pl.small[:, 2:3], 1.0)

        @block.scalar
        def _(act):
            act.activation(pl.csil[:, :, :], pl.cin[:, :, :], ACT.Silu)



def modulation(pl, l):
    nc, a = pl.nc, pl.a
    slots, per = 4, 4
    w = [pl.at(f"wada{l}_{s}", [P, KT, per * P], F32, kb=16 * s) for s in range(slots)]
    loaded = [pl.sem(f"ada_loaded{l}_{s}") for s in range(slots)]
    prm_in = pl.sem(f"prm_in{l}")
    used = pl.sem(f"ada_used{l}")
    evicted = pl.sem(f"ada_evicted{l}")
    n_iter = 48 // per // slots
    with nc.Block() as block:
        @block.sync
        def _(sp):
            sp.dma_start(pl.prm[:, :], a["prm"][l]).then_inc(prm_in, 16)
            sp.sem_inc(used, slots)
            with sp.Fori(0, n_iter) as i:
                for s in range(slots):
                    sp.wait_ge(used, i * slots + (s + 1))
                    sp.dma_start(w[s][:, :, :], a["w_ada"][l, i * slots + s]).then_inc(loaded[s], 16)

        @block.tensor
        def _(pe):
            pe.sem_inc(evicted, 2)
            with pe.Fori(0, n_iter) as i:
                for s in range(slots):
                    pe.wait_ge(loaded[s], i * 16 + 16)
                    pe.wait_ge(evicted, i * slots + (s + 1))
                    for t in range(per):
                        for k in range(KT):
                            mm = pe.matmul(pl.ps[:, 512 * (s % 2) + 2 * t:512 * (s % 2) + 2 * t + 2],
                                           w[s][:, k, t * P:(t + 1) * P], pl.csil[:, k, :],
                                           start=(k == 0), stop=(k == KT - 1))
                    mm.then_inc(used, 1)

        @block.vector
        def _(dve):
            dve.wait_ge(prm_in, 16)
            with dve.Fori(0, n_iter) as i:
                for s in range(slots):
                    dve.wait_ge(used, i * slots + (s + 1 + slots))
                    bias = pl.prm[:, BADA:BADA + 48].rearrange("p (b t) -> p b t", t=per)
                    dst = pl.mod[:, :, :].rearrange("p (b t) c -> p b t c", t=per)
                    src = pl.ps[:, 512 * (s % 2):512 * (s % 2) + 2 * per].rearrange("p (t c) -> p t c", c=2)
                    dve.tensor_tensor(dst[:, i * slots + s], src,
                                      bias[:, i * slots + s, :].unsqueeze(2).broadcast_to([P, per, 2]),
                                      ALU.add).then_inc(evicted, 1)
            dve.wait_ge(evicted, 48 // per + 2)
            for sc in (SC1, SC2):
                dve.tensor_scalar(pl.mod[:, sc:sc + KT, :], pl.mod[:, sc:sc + KT, :], 1.0, None, ALU.add)



def modulate(pl, l, which, sc, sh, chunks, spill):
    nc = pl.nc
    tmp = [pl.at(f"modt{l}{which}{s}", [P, TOK], F32, kb=150 + 5 * s) for s in range(2)]
    scaled = pl.sem(f"mod_scaled{l}{which}")
    rounded = pl.sem(f"mod_rounded{l}{which}")
    rest = pl.sem(f"mod_rest{l}{which}")
    spilled = pl.sem(f"mod_spilled{l}{which}")
    width = TOK if 2 in chunks else SEQ
    with nc.Block() as block:
        if spill:
            @block.sync
            def _(sp):
                sp.dma_start(pl.x_dram, pl.x[:, :, :]).then_inc(spilled, 16)
                sp.wait_ge(spilled, 16)

        @block.vector
        def _(dve):
            with dve.Fori(0, KT // 2) as i:
                for s in range(2):
                    k = i * 2 + s
                    dve.wait_ge(rest, i * 2 + (s + 1))
                    ins = dve.tensor_scalar(tmp[s][:, 0:SEQ], pl.x[:, k, 0:SEQ], pl.mod[:, k + sc, 0:1],
                                            pl.mod[:, k + sh, 0:1], ALU.mult, ALU.add)
                    if 2 in chunks:
                        ins = dve.tensor_scalar(tmp[s][:, SEQ:TOK], pl.x[:, k, SEQ:TOK],
                                                pl.mod[:, k + sc, 1:2], pl.mod[:, k + sh, 1:2],
                                                ALU.mult, ALU.add)
                    ins.then_inc(scaled, 1)

        @block.scalar
        def _(act):
            with act.Fori(0, KT // 2) as i:
                for s in range(2):
                    act.wait_ge(scaled, i * 2 + (s + 1))
                    act.activation(pl.hi[:, i * 2 + s, 0:width], tmp[s][:, 0:width], ACT.Copy) \
                        .then_inc(rounded, 1)

        @block.gpsimd
        def _(pool):
            pool.sem_inc(rest, 2)
            with pool.Fori(0, KT // 2) as i:
                for s in range(2):
                    k = i * 2 + s
                    pool.wait_ge(rounded, i * 2 + (s + 1))
                    pool.tensor_tensor(pl.lo[:, k, 0:width], tmp[s][:, 0:width],
                                       raw(pl.hi[:, k, 0:width]), ALU.subtract).then_inc(rest, 1)



class Ring:

    def __init__(self, pl, tag, kb=167):
        self.raw = [pl.at(f"wraw{tag}{s}", [P, D], F32, kb=kb + 4 * s) for s in range(2)]
        self.hi = [pl.at(f"whi{tag}{s}", [P, KT, P], F32R, kb=kb + 8 + 4 * s) for s in range(2)]
        self.lo = [pl.at(f"wlo{tag}{s}", [P, KT, P], F32R, kb=kb + 16 + 4 * s) for s in range(2)]
        self.one = pl.small[:, 2:3].broadcast_to([P, D])
        self.loaded = [pl.sem(f"w_loaded{tag}{s}") for s in range(2)]
        self.rounded = pl.sem(f"w_rounded{tag}")
        self.ready = pl.sem(f"w_ready{tag}")

    def load(self, sp, at, src):
        sp.wait_ge(self.ready, at.n + 1)
        sp.dma_start(self.raw[at.par][:, :], src).then_inc(self.loaded[at.par], 16)

    def split(self, pool, at, done):
        w, hi, lo = self.raw[at.par][:, :], self.hi[at.par], self.lo[at.par]
        hi, lo = (t[:, :, :].rearrange("p k n -> p (k n)") for t in (hi, lo))
        pool.wait_ge(self.loaded[at.par], at.half * 16 + 16)
        pool.wait_ge(done, at.n + 1)
        pool.tensor_tensor(hi, w, self.one, ALU.mult).then_inc(self.rounded, 1)
        pool.wait_ge(self.rounded, at.n + 1)
        pool.tensor_tensor(lo, w, raw(hi), ALU.subtract).then_inc(self.ready, 1)


def multiply_block(pl, pe, ring, at, chunks, full, taken):
    pe.wait_ge(ring.ready, at.n + 3)
    for c in ORDER:
        if c in chunks:
            t0, tn = CHUNKS[c]
            pe.wait_ge(taken[c], at.number(c) + 1)
            for k in range(KT):
                mm = three_pass(pe, pl.bank(3 * at.par + c, tn), ring.hi[at.par][:, k, :],
                                ring.lo[at.par][:, k, :], pl.hi[:, k, t0:t0 + tn],
                                pl.lo[:, k, t0:t0 + tn], k == 0, k == KT - 1)
            mm.then_inc(full[c], 1)


def wait_full(eng, full, at, c):
    eng.wait_ge(full[c], at.number(c) + (3 if c == 1 else 1))


PADDED = (2, 514, SEQ + 6)


def transpose_chunk(pl, pe, src, c, bank):
    for t in range(CHUNKS[c][1] // P):
        p0 = PADDED[c] + t * P
        tr = pe.transpose(pl.bank(bank)[:, t * P:(t + 1) * P], src[:, p0:p0 + P], pl.c(IDENT))
    return tr



def project_attention(pl, l, last):
    nc, a = pl.nc, pl.a
    tag = f"ab{l}"
    chunks_of = lambda kind: (0, 1) if last and kind in ("q0", "q1") else ORDER
    segments = [(2, ["q0", "q1", "k", "v"])]
    ring = Ring(pl, tag)
    full = [pl.sem(f"{tag}_full{c}") for c in range(3)]
    taken = [pl.sem(f"{tag}_taken{c}") for c in range(3)]
    vst = pl.at(f"{tag}_vst", [P, TOK + 8], F32, kb=150)
    turned = pl.sem(f"{tag}_turned")
    stored = pl.sem(f"{tag}_stored")
    with nc.Block() as block:
        @block.sync
        def _(sp):
            over(sp, segments, chunks_of, lambda at: ring.load(sp, at, a["w_in"][l, at.n]))

        @block.gpsimd
        def _(pool):
            pool.sem_inc(ring.ready, 2)
            over(pool, segments, chunks_of, lambda at: ring.split(pool, at, full[1]))

        @block.tensor
        def _(pe):
            pe.sem_inc(full[1], 2)

            def body(at):
                multiply_block(pl, pe, ring, at, chunks_of(at.kind), full, taken)
                if at.kind == "v":
                    for g, c in enumerate(ORDER):
                        pe.wait_ge(taken[c], at.number(c) + 3)
                        pe.wait_ge(stored, at.i * 3 + (g + 1 if g < 2 else 2))
                        transpose_chunk(pl, pe, vst, c, 6 + g % 2).then_inc(turned, 1)
            over(pe, segments, chunks_of, body)

        @block.scalar
        def _(act):
            for c in range(3):
                act.sem_inc(taken[c], 2)

            def body(at):
                for c in ORDER:
                    if c not in chunks_of(at.kind):
                        continue
                    t0, tn = CHUNKS[c]
                    wait_full(act, full, at, c)
                    if at.kind == "v":
                        dst = vst[:, PADDED[c]:PADDED[c] + tn]
                    else:
                        dst = pl.qk[:, at.i * 3 + at.j, t0:t0 + tn]
                    act.activation(dst, pl.bank(3 * at.par + c, tn), ACT.Copy).then_inc(taken[c], 1)
            over(act, segments, chunks_of, body)

        @block.vector
        def _(dve):
            dve.sem_inc(stored, 1)
            with dve.Fori(0, 2) as i:
                for g, c in enumerate(ORDER):
                    t0, tn = CHUNKS[c]
                    dve.wait_ge(turned, i * 3 + (g + 1))
                    dve.tensor_copy(pl.v[:, t0 // P:(t0 + tn) // P, :].rearrange("p t (g d) -> p t g d", g=2)[:, :, i, :],
                                    pl.bank(6 + g % 2, tn).rearrange("p (t d) -> p t d", d=P)) \
                        .then_inc(stored, 1)



def norm_and_rotate(pl, l, last):
    nc = pl.nc
    tag = f"nr{l}"
    norms = [(t, c) for t in (3, 4, 5) for c in ORDER if not (last and t < 5 and c == 2)]
    turns = [(t, c) for t in range(6) for c in (0, 1)]
    rope = pl.at(f"{tag}_rope", [P, 2, SEQ], F32, kb=161)
    sq = [pl.at(f"{tag}_sq{s}", [P, 512], F32, kb=169 + 2 * s) for s in range(2)]
    rt = [pl.at(f"{tag}_rt{s}", [P, 512], F32, kb=173 + 2 * s) for s in range(2)]
    ri = [pl.at(f"{tag}_ri{s}", [P, 512], F32, kb=177 + 2 * s) for s in range(2)]
    xc = [pl.at(f"{tag}_xc{s}", [P, 512], F32, kb=181 + 2 * s) for s in range(2)]
    xs = [pl.at(f"{tag}_xs{s}", [P, 512], F32, kb=185 + 2 * s) for s in range(2)]
    table = pl.sem(f"{tag}_table")
    squared, summed, rooted, inverted, normed = (pl.sem(f"{tag}_{x}") for x in
                                                 ("squared", "summed", "rooted", "inverted", "normed"))
    with_cos, rotated, with_sin, done = (pl.sem(f"{tag}_{x}") for x in
                                         ("with_cos", "rotated", "with_sin", "done"))
    N = len(norms)

    def normed_before(t):
        return sum(1 for u, _ in norms if u <= t)

    with nc.Block() as block:
        @block.sync
        def _(sp):
            sp.dma_start(rope[:, :, :], pl.a["rope"]).then_inc(table, 16)
            sp.wait_ge(table, 16)

        @block.scalar
        def _(act):
            def square(n):
                t, c = norms[n]
                t0, tn = CHUNKS[c]
                if n >= 2:
                    act.wait_ge(summed, n - 1)
                act.activation(sq[n % 2][:, 0:tn], pl.qk[:, t, t0:t0 + tn], ACT.Square) \
                    .then_inc(squared, 1)
            square(0)
            for n, (t, c) in enumerate(norms):
                if n + 1 < N:
                    square(n + 1)
                tn = CHUNKS[c][1]
                act.wait_ge(summed, n + 1)
                if n >= 2:
                    act.wait_ge(inverted, n - 1)
                act.activation(rt[n % 2][:, 0:tn], pl.bank(n % 2, tn), ACT.Sqrt,
                               bias=pl.small[:, 0:1]).then_inc(rooted, 1)

        @block.tensor
        def _(pe):
            for n, (t, c) in enumerate(norms):
                tn = CHUNKS[c][1]
                pe.wait_ge(squared, n + 1)
                if n >= 2:
                    pe.wait_ge(rooted, n - 1)
                pe.matmul(pl.bank(n % 2, tn), pl.c(BLOCK64), sq[n % 2][:, 0:tn], start=True,
                          stop=True).then_inc(summed, 1)
            for n, (t, c) in enumerate(turns):
                t0, tn = CHUNKS[c]
                if t >= 3:
                    pe.wait_ge(normed, normed_before(t))
                if n >= 2:
                    pe.wait_ge(with_sin, n - 1)
                pe.matmul(pl.bank(2 + n % 2, tn), pl.c(ROT), pl.qk[:, t, t0:t0 + tn], start=True,
                          stop=True).then_inc(rotated, 1)

        @block.gpsimd
        def _(pool):
            pool.wait_ge(table, 16)
            for n, (t, c) in enumerate(turns):
                t0, tn = CHUNKS[c]
                if t >= 3:
                    pool.wait_ge(normed, normed_before(t))
                if n >= 2:
                    pool.wait_ge(done, n - 1)
                pool.tensor_tensor(xc[n % 2][:, :], pl.qk[:, t, t0:t0 + tn], rope[:, 0, t0:t0 + tn],
                                   ALU.mult).then_inc(with_cos, 1)

        @block.vector
        def _(dve):
            for n, (t, c) in enumerate(norms):
                t0, tn = CHUNKS[c]
                gain = pl.prm[:, (KGAIN if t == 5 else QGAIN):(KGAIN if t == 5 else QGAIN) + 1]
                dve.wait_ge(rooted, n + 1)
                dve.reciprocal(ri[n % 2][:, 0:tn], rt[n % 2][:, 0:tn]).then_inc(inverted, 1)
                dve.wait_ge(inverted, n + 1)
                x = pl.qk[:, t, t0:t0 + tn]
                dve.scalar_tensor_tensor(out=x, in0=x, scalar=gain, in1=ri[n % 2][:, 0:tn],
                                         op0=ALU.mult, op1=ALU.mult).then_inc(normed, 1)
            dve.wait_ge(table, 16)
            for n, (t, c) in enumerate(turns):
                t0, tn = CHUNKS[c]
                dve.wait_ge(rotated, n + 1)
                dve.tensor_tensor(xs[n % 2][:, :], pl.bank(2 + n % 2, tn), rope[:, 1, t0:t0 + tn],
                                  ALU.mult).then_inc(with_sin, 1)
                dve.wait_ge(with_sin, n + 1)
                dve.wait_ge(with_cos, n + 1)
                dve.tensor_tensor(pl.qk[:, t, t0:t0 + tn], xc[n % 2][:, :], xs[n % 2][:, :], ALU.add) \
                    .then_inc(done, 1)



def attend(pl, l, last):
    nc = pl.nc
    tag = f"at{l}"
    tiles = LT if last else TT
    blocks = [("A" if i < LT else "C", i, 0) for i in range(tiles)] + \
             [("B" if i < LT else "C", i, 1) for i in range(tiles)]
    n_keys = {"A": 5, "B": TT, "C": 2}
    groups = {"A": ((0, 4), (4, 5)), "B": ((0, 4), (4, 8), (8, 10)), "C": ((0, 2),)}
    segments = [(0, 1), (1, 2), (2, 6), (6, 7), (7, 8)] + [(i, i + 1) for i in range(8, tiles)]
    segments += [(tiles, tiles + 1), (tiles + 1, tiles + 7), (tiles + 7, tiles + 8)]
    segments += [(i, i + 1) for i in range(tiles + 8, 2 * tiles)]
    late = [0]
    for kind, _, _ in blocks:
        late.append(late[-1] + HEADS * (len(groups[kind]) - 1))

    prob = [pl.at(f"{tag}_prob{s}", [P, TOK], F32, kb=161 + 5 * s) for s in range(2)]
    turned = [pl.at(f"{tag}_turned{s}", [P, TOK], F32, kb=171 + 5 * s) for s in range(2)]
    qst = pl.at(f"{tag}_qst", [P, HEADS, P], F32, kb=181)
    st = pl.at(f"{tag}_st", [P, 64], F32, kb=183)
    mx, nm, es, den, dn, rd = ([st[:, HEADS * j + h:HEADS * j + h + 1] for h in range(HEADS)]
                               for j in range(6))
    nsink = st[:, 6 * HEADS:7 * HEADS]

    s_full, masked, maxed, nm_done, p_done, es_done, dn_done, rd_done, q_ready, nsink_done = (
        pl.sem(f"{tag}_{x}") for x in ("s_full", "masked", "maxed", "nm_done", "p_done", "es_done",
                                       "dn_done", "rd_done", "q_ready", "nsink_done"))
    t_full, first_copied, later_copied, pv_done, o_done = (
        pl.sem(f"{tag}_{x}") for x in ("t_full", "first_copied", "later_copied", "pv_done", "o_done"))

    class Unit:

        def __init__(self, r, b, h):
            self.kind, _, self.group = blocks[r]
            self.h, self.b, self.r = h, b, r
            self.i = b if self.group == 0 else b - tiles
            self.static = isinstance(b, int)
            self.u = b * HEADS + h
            self.par = h % 2
            per = len(groups[self.kind]) - 1
            self.late = (b - r) * (HEADS * per) + (late[r] + h * per)
            self.all = self.late + self.u

        def step(self, d):
            h = self.h + d
            if h in range(HEADS):
                return Unit(self.r, self.b, h)
            r = self.r + (1 if d > 0 else -1)
            if r not in range(len(blocks)):
                return None
            return Unit(r, self.b + (1 if d > 0 else -1), h % HEADS)

        def keys(self):
            if self.kind == "A":
                i = self.i
                window = [max(i - 1, 0), i, min(i + 1, LT - 1)] if self.static else [i - 1, i, i + 1]
                return window + [LT, LT + 1]
            return list(range(TT)) if self.kind == "B" else [LT, LT + 1]

        def runs(self):
            k = self.keys()
            if self.kind == "B":
                return [(0, 0, 4), (4, 4, 4), (8, 8, 2)]
            if self.kind == "C":
                return [(0, LT, 2)]
            if self.static and self.i == 0:
                window = [(0, 0, 1), (1, 0, 2)]
            elif self.static and self.i == LT - 1:
                window = [(0, LT - 2, 2), (2, LT - 1, 1)]
            else:
                window = [(0, k[0], 3)]
            return window + [(3, LT, 1), (4, LT + 1, 1)]

        def scores(self, t0=0, n=None):
            n = n_keys[self.kind] if n is None else n
            return pl.ps[:, 1536 * self.par + t0 * P:1536 * self.par + (t0 + n) * P]

    def over_units(eng, body):
        for lo, hi in segments:
            if hi - lo > 1:
                with eng.Fori(lo, hi) as b:
                    for h in range(HEADS):
                        body(Unit(lo, b, h))
            else:
                for h in range(HEADS):
                    body(Unit(lo, lo, h))

    final = Unit(len(blocks) - 1, len(blocks) - 1, HEADS - 1)

    with nc.Block() as block:
        @block.gpsimd
        def _(pool):
            for p0 in (0, HD):
                h0 = 2 - 2 * (p0 // HD)
                pool.memset(qst[p0:p0 + HD, h0:h0 + 2, :], 0.0).then_inc(q_ready, 1)
            for lo, hi in segments:
                def stage(b):
                    g = blocks[lo][2]
                    i = b - g * tiles
                    if not (isinstance(b, int) and b == 0):
                        pool.wait_ge(s_full, b * HEADS)
                    src = pl.qk[:, 3 * g:3 * g + 2, :].rearrange("p k (t q) -> p k t q", q=P)
                    for p0 in (0, HD):
                        h0 = 2 * (p0 // HD)
                        pool.tensor_copy(qst[p0:p0 + HD, h0:h0 + 2, :], src[p0:p0 + HD, :, i, :]) \
                            .then_inc(q_ready, 1)
                if hi - lo > 1:
                    with pool.Fori(lo, hi) as b:
                        stage(b)
                else:
                    stage(lo)

        @block.tensor
        def _(pe):
            def score(w):
                if w.h == 0:
                    pe.wait_ge(q_ready, w.b * 2 + 4)
                if not (w.static and w.u < 2):
                    pe.wait_ge(p_done, w.u - 1)
                ktile = pl.qk[:, 3 * w.group + 2, :].rearrange("p (t k) -> p t k", k=P)
                runs = w.runs()
                for place, tile, n in runs:
                    out = w.scores(place, n).rearrange("p (t k) -> p t k", k=P)
                    mm = pe.matmul(out, qst[:, w.h, :], ktile[:, bass.ds(tile, n), :],
                                   start=True, stop=True)
                mm.then_inc(s_full, 1)

            def transposes(w, g):
                first, end = groups[w.kind][g]
                if g == 0:
                    pe.wait_ge(p_done, w.u + 1)
                if g == 0:
                    v = w.step(-1)
                    if v is not None and len(groups[v.kind]) == 1:
                        pe.wait_ge(first_copied, w.u)
                    elif v is not None:
                        pe.wait_ge(later_copied, w.late)
                elif g == 1:
                    pe.wait_ge(first_copied, w.u + 1)
                else:
                    pe.wait_ge(later_copied, w.late + (g - 1))
                for t in range(first, end):
                    tr = pe.transpose(pl.bank(6)[:, (t - first) * P:(t - first + 1) * P],
                                      prob[w.par][:, t * P:(t + 1) * P], pl.c(IDENT))
                tr.then_inc(t_full, 1)

            def values(w, g):
                first, end = groups[w.kind][g]
                if g == 0:
                    pe.wait_ge(first_copied, w.u + 1)
                    if not (w.static and w.u < 1):
                        pe.wait_ge(o_done, w.u)
                else:
                    pe.wait_ge(later_copied, w.late + g)
                keys = w.keys()
                col = 128 * w.group + HD * (w.h // 2)
                for t in range(first, end):
                    mm = pe.matmul(pl.bank(7, HD), turned[w.par][:, t * P:(t + 1) * P],
                                   pl.v[:, keys[t], col:col + HD], start=(t == 0),
                                   stop=(t == len(keys) - 1))
                if end == len(keys):
                    mm.then_inc(pv_done, 1)

            score(Unit(0, 0, 0))

            def body(w):
                nxt, prev = w.step(1), w.step(-1)
                if nxt is not None:
                    score(nxt)
                for g in range(len(groups[w.kind])):
                    transposes(w, g)
                    if prev is not None and g < len(groups[prev.kind]):
                        values(prev, g)
                if prev is not None:
                    for g in range(len(groups[w.kind]), len(groups[prev.kind])):
                        values(prev, g)
            over_units(pe, body)
            for g in range(len(groups[final.kind])):
                values(final, g)

        @block.vector
        def _(dve):
            def maximum(w):
                dve.wait_ge(s_full, w.u + 1)
                if w.kind == "A":
                    if w.static:
                        variant = 0 if w.i == 0 else 2 if w.i == LT - 1 else 1
                    else:
                        variant = 1
                    win = w.scores(0, 3)
                    dve.tensor_tensor(win, win, pl.c(MASKS + 3 * P * variant, 3 * P), ALU.add) \
                        .then_inc(masked, 1)
                    dve.wait_ge(masked, w.u + 1)
                dve.tensor_reduce(mx[w.h], w.scores(), AX.X, ALU.max).then_inc(maxed, 1)
                dve.wait_ge(maxed, w.u + 1)
                if w.group == 0:
                    dve.tensor_scalar(nm[w.h], mx[w.h], -SCALE, nsink[:, w.h:w.h + 1],
                                      ALU.mult, ALU.min).then_inc(nm_done, 1)
                else:
                    dve.tensor_scalar(nm[w.h], mx[w.h], -SCALE, None, ALU.mult).then_inc(nm_done, 1)

            def copy_first(w):
                end = groups[w.kind][0][1]
                dve.wait_ge(t_full, w.all + 1)
                dve.tensor_copy(turned[w.par][:, 0:end * P], pl.bank(6, end * P)).then_inc(first_copied, 1)

            def output(w):
                if w.group == 0:
                    dve.wait_ge(es_done, w.u + 1)
                    dve.tensor_tensor(dn[w.h], den[w.h], es[w.h], ALU.add).then_inc(dn_done, 1)
                    dve.wait_ge(dn_done, w.u + 1)
                    dve.reciprocal(rd[w.h], dn[w.h]).then_inc(rd_done, 1)
                else:
                    dve.reciprocal(rd[w.h], den[w.h]).then_inc(rd_done, 1)
                dve.wait_ge(rd_done, w.u + 1)
                dve.wait_ge(pv_done, w.u + 1)
                col = HEADS * HD * w.group + HD * w.h
                dve.tensor_scalar(pl.mixab[:, w.i, col:col + HD], pl.bank(7, HD), rd[w.h], None,
                                  ALU.mult).then_inc(o_done, 1)

            dve.tensor_scalar(nsink, pl.prm[:, SINK:SINK + HEADS], -1.0, None, ALU.mult) \
                .then_inc(nsink_done, 1)
            dve.wait_ge(nsink_done, 1)
            maximum(Unit(0, 0, 0))

            def body(w):
                nxt, prev = w.step(1), w.step(-1)
                copy_first(w)
                if nxt is not None:
                    maximum(nxt)
                if prev is not None:
                    output(prev)
            over_units(dve, body)
            output(final)

        @block.scalar
        def _(act):
            def exponent(w):
                act.wait_ge(nm_done, w.u + 1)
                if not (w.static and w.u < 2):
                    act.wait_ge(t_full, w.step(-1).all)
                if not (w.static and w.u < HEADS):
                    act.wait_ge(o_done, w.u - (HEADS - 1))
                if w.group == 0:
                    act.activation(es[w.h], pl.prm[:, SINK + w.h:SINK + w.h + 1], ACT.Exp,
                                   bias=nm[w.h]).then_inc(es_done, 1)
                act.activation(prob[w.par][:, 0:n_keys[w.kind] * P], w.scores(), ACT.Exp, bias=nm[w.h],
                               scale=SCALE, accum_out=den[w.h]).then_inc(p_done, 1)

            exponent(Unit(0, 0, 0))

            def body(w):
                nxt = w.step(1)
                for g in range(1, len(groups[w.kind])):
                    first, end = groups[w.kind][g]
                    act.wait_ge(t_full, w.all + (g + 1))
                    act.activation(turned[w.par][:, first * P:end * P], pl.bank(6, (end - first) * P),
                                   ACT.Copy).then_inc(later_copied, 1)
                if nxt is not None:
                    exponent(nxt)
            over_units(act, body)



def project_ssd(pl, l, last):
    nc, a = pl.nc, pl.a
    tag = f"c{l}"
    kinds = ["z"] * 4 + ["x"] * 4 + ["b"] * 2 + ["s"] * 2 + ["dt"]
    chunks_of = lambda kind: (0, 1) if last and kind == "z" else ORDER
    order_of = lambda kind: [c for c in ORDER if c in chunks_of(kind)]
    segments = [(1, kinds[2 * n:2 * n + 2]) for n in range(7)]
    ring = Ring(pl, tag)
    full = [pl.sem(f"{tag}_full{c}") for c in range(3)]
    taken = [pl.sem(f"{tag}_taken{c}") for c in range(3)]
    pad = [pl.at(f"{tag}_pad{s}", [P, TOK + 8], F32, kb=150 + 5.25 * s) for s in range(2)]
    u = pl.at(f"{tag}_u", [P, TOK], F32, kb=161)
    zs = pl.at(f"{tag}_zs", [P, TT, P], F32, kb=161)
    cleared = pl.sem(f"{tag}_cleared")
    tapped = pl.sem(f"{tag}_tapped")
    smooth = pl.sem(f"{tag}_smooth")
    turned = pl.sem(f"{tag}_turned")
    stored = pl.sem(f"{tag}_stored")
    z_out = pl.sem(f"{tag}_z_out")

    turns = {n: [] for n in range(13)}
    for n, kind in enumerate(kinds):
        of = n if kind in ("z", "dt") else n - 1
        if of >= 0 and (of == n or kinds[of] in ("x", "b")):
            turns[n] = [(of, c) for c in order_of(kinds[of])]
    flat = [x for n in range(13) for x in turns[n]]
    number = {x: q for q, x in enumerate(flat)}
    through = {of: max(q for x, q in number.items() if x[0] == of) + 1 for of, _ in flat}
    parts = ((SEQ, CTX, (2,)), (0, 510, (0,)), (510, 514, (0, 1)))
    per_block = len(parts) * CONV

    def count(of, c):
        return sum(c in chunks_of(k) for k in kinds[:of + 1])

    with nc.Block() as block:
        @block.sync
        def _(sp):
            def z_store(n):
                sp.wait_ge(stored, through[n] + 2)
                width = SEQ // P if last else TT
                sp.dma_start(pl.z_dram[:, 0:width, n * P:(n + 1) * P], zs[:, 0:width, :]) \
                    .then_inc(z_out, 16)

            def body(at):
                ring.load(sp, at, a["w_in"][l, 8 + at.n])
                if 2 <= at.n < 6:
                    z_store(at.n - 2)
            over(sp, segments, chunks_of, body)
            sp.wait_ge(z_out, 64)

        @block.gpsimd
        def _(pool):
            pool.sem_inc(ring.ready, 2)
            for s in range(2):
                pool.memset(pad[s][:, 0:2], 0.0)
                pool.memset(pad[s][:, SEQ + 2:SEQ + 6], 0.0)
                pool.memset(pad[s][:, TOK + 6:TOK + 8], 0.0).then_inc(cleared, 1)
            over(pool, segments, chunks_of, lambda at: ring.split(pool, at, full[1]))

        @block.tensor
        def _(pe):
            pe.sem_inc(full[1], 2)

            def body(at):
                multiply_block(pl, pe, ring, at, chunks_of(at.kind), full, taken)
                for of, c in turns[at.n]:
                    q = number[of, c]
                    if kinds[of] in ("z", "dt"):
                        src = pad[of % 2]
                        pe.wait_ge(taken[c], count(of, c) + 2)
                    else:
                        pe.wait_ge(smooth, of - 3)
                    pe.wait_ge(stored, q + 1)
                    for t in range(CHUNKS[c][1] // P):
                        tok = CHUNKS[c][0] + t * P
                        if kinds[of] in ("z", "dt"):
                            src = pad[of % 2][:, PADDED[c] + t * P:PADDED[c] + (t + 1) * P]
                        elif kinds[of] == "x":
                            src = u[:, tok:tok + P]
                        else:
                            src = pl.bt[:, of - 8, tok:tok + P]
                        tr = pe.transpose(pl.bank(6 + q % 2)[:, t * P:(t + 1) * P], src, pl.c(IDENT))
                    tr.then_inc(turned, 1)
            over(pe, segments, chunks_of, body)


        @block.scalar
        def _(act):
            for c in range(3):
                act.sem_inc(taken[c], 2)
            act.sem_inc(stored, 2)

            def take(at, c):
                if c not in chunks_of(at.kind):
                    return
                tn = CHUNKS[c][1]
                wait_full(act, full, at, c)
                if at.n >= 6 and at.n < 12:
                    act.wait_ge(tapped, (at.n - 5) * per_block)
                elif at.n == 12:
                    act.wait_ge(tapped, 7 * per_block)
                act.activation(pad[at.par][:, PADDED[c]:PADDED[c] + tn], pl.bank(3 * at.par + c, tn),
                               ACT.Silu if at.kind == "z" else ACT.Copy).then_inc(taken[c], 1)

            def store(of, c):
                q = number[of, c]
                t0, tn = CHUNKS[c]
                tt = slice(t0 // P, (t0 + tn) // P)
                act.wait_ge(turned, q + 1)
                src = pl.bank(6 + q % 2, tn).rearrange("p (t d) -> p t d", d=P)
                if kinds[of] == "z":
                    if of >= 1:
                        act.wait_ge(z_out, 16 * of)
                    dst = zs[:, tt, :]
                elif kinds[of] == "dt":
                    dst, src = pl.dtr[:, tt, :], src[:, :, P - 2 * CH:P]
                else:
                    dst = pl.xb[:, tt, (of - 4) * P:(of - 3) * P]
                act.activation(dst, src, ACT.Copy).then_inc(stored, 1)

            def body(at):
                take(at, 2)
                take(at, 0)
                if at.n >= 5:
                    m = at.n - 5
                    act.wait_ge(tapped, (m + 1) * per_block)
                    kind = kinds[at.n - 1]
                    dst = u[:, :] if kind == "x" else pl.bt[:, m - 4, :] if kind == "b" else pl.ct[:, m - 6, :]
                    act.activation(dst, u[:, :], ACT.Silu).then_inc(smooth, 1)
                take(at, 1)
                for of, c in turns[at.n]:
                    store(of, c)
            over(act, segments, chunks_of, body)

        @block.vector
        def _(dve):
            dve.wait_ge(cleared, 2)
            dve.wait_ge(z_out, 64)
            for m in range(8):
                n = m + 4
                w = pl.prm[:, CONVW + CONV * m:CONVW + CONV * (m + 1)]
                if m >= 1:
                    if kinds[n - 1] == "x":
                        dve.wait_ge(turned, through[n - 1])
                    else:
                        dve.wait_ge(smooth, m)
                for j in range(CONV):
                    for q, (t0, tn, need) in enumerate(parts):
                        if j == 0:
                            for c in need:
                                dve.wait_ge(taken[c], count(n, c) + 2)
                        s0 = t0 + j + (4 if t0 == SEQ else 0)
                        src, out = pad[n % 2][:, s0:s0 + tn], u[:, t0:t0 + tn]
                        if j == 0:
                            dve.tensor_scalar(out, src, w[:, 0:1], pl.prm[:, CONVB + m:CONVB + m + 1],
                                              ALU.mult, ALU.add).then_inc(tapped, 1)
                        else:
                            dve.wait_ge(tapped, m * per_block + (j - 1) * len(parts) + q + 1)
                            dve.scalar_tensor_tensor(out=out, in0=src, scalar=w[:, j:j + 1], in1=out,
                                                     op0=ALU.mult, op1=ALU.add).then_inc(tapped, 1)



def scan(pl, l, last):
    nc = pl.nc
    tag = f"s{l}"
    at = pl.at
    hb = at(f"{tag}_hb", [P, TT + 1, 512], F32, kb=0)
    zt = [at(f"{tag}_z{s}", [P, 512], F32, kb=22 + 2 * s) for s in range(2)]
    up_f, up_b = (at(f"{tag}_up{d}", [P, CH, P], F32, kb=26 + 4 * d) for d in range(2))
    e_f, e_b = (at(f"{tag}_e{d}", [P, CH, P], F32, kb=34 + 4 * d) for d in range(2))
    xd_f, xd_b, xfe = (at(f"{tag}_xd{d}", [P, 512], F32, kb=42 + 2 * d) for d in range(3))
    hf = [at(f"{tag}_hf{s}", [P, 512], F32, kb=48 + 2 * s) for s in range(2)]
    b_st, c_st, b_tok = (at(f"{tag}_st{d}", [P, GROUPS, P], F32, kb=52 + d) for d in range(3))
    g_f, g_b = (at(f"{tag}_g{d}", [P, GROUPS, P], F32, kb=55 + d) for d in range(2))
    t1, t2, xskip = (at(f"{tag}_t{d}", [P, 512], F32, kb=57 + 2 * d) for d in range(3))
    dt, dta, dend, eac, cdec, wde, tmp, tmp2, tmp3 = (
        at(f"{tag}_d{d}", [P, TT, 2 * CH], F32, kb=63 + 0.625 * d) for d in range(9))
    av = at(f"{tag}_av", [P, 2 * CH], F32, kb=69)
    xde = [at(f"{tag}_xde{s}", [P, 512], F32, kb=70 + 2 * s) for s in range(2)]
    b_tok1 = [at(f"{tag}_bt{s}", [P, 256], F32, kb=74 + s) for s in range(2)]
    sq = at(f"{tag}_sq", [P, 512], F32, kb=76)
    FW, BW = slice(0, CH), slice(CH, 2 * CH)

    def sem(name):
        return pl.sem(f"{tag}_{name}")
    step, summed, acted = sem("step"), sem("summed"), sem("acted")

    def heads(t):
        return t.rearrange("p (h d) -> p h d", h=CH)

    def per_head(t, c, cols):
        return t[:, c, cols].unsqueeze(2).broadcast_to([P, CH, HD])

    with nc.Block() as block:
        @block.vector
        def _(dve):
            done = [0]

            def chain(ins):
                done[0] += 1
                ins.then_inc(step, 1)
                dve.wait_ge(step, done[0])
            bias = pl.prm[:, DTB:DTB + 2 * CH].unsqueeze(1).broadcast_to([P, TT, 2 * CH])
            chain(dve.tensor_tensor(tmp[:, :, :], pl.dtr[:, :, :], bias, ALU.add))
            chain(dve.scalar_tensor_tensor(out=tmp2[:, :, :], in0=tmp[:, :, :], scalar=-1.0,
                                           in1=tmp[:, :, :], op0=ALU.mult, op1=ALU.max))
            dve.wait_ge(acted, 1)
            chain(dve.tensor_scalar(tmp2[:, :, :], tmp3[:, :, :], 1.0, None, ALU.add))
            chain(dve.tensor_scalar(dend[:, :, :], tmp2[:, :, :], -1.0, None, ALU.add))
            chain(dve.tensor_tensor(dend[:, :, :], tmp3[:, :, :], dend[:, :, :], ALU.subtract))
            chain(dve.reciprocal(eac[:, :, :], tmp2[:, :, :]))
            chain(dve.tensor_tensor(dend[:, :, :], dend[:, :, :], eac[:, :, :], ALU.mult))
            dve.wait_ge(acted, 2)
            chain(dve.tensor_tensor(dend[:, :, :], dend[:, :, :], cdec[:, :, :], ALU.add))
            chain(dve.scalar_tensor_tensor(out=dt[:, :, :], in0=tmp[:, :, :], scalar=0.0,
                                           in1=dend[:, :, :], op0=ALU.max, op1=ALU.add))
            dve.wait_ge(acted, 3)
            chain(dve.scalar_tensor_tensor(out=dta[:, :, :], in0=dt[:, :, :], scalar=-1.0,
                                           in1=av[:, :].unsqueeze(1).broadcast_to([P, TT, 2 * CH]),
                                           op0=ALU.mult, op1=ALU.mult))
            dve.wait_ge(acted, 8)
            dve.tensor_tensor(wde[:, :, :], dt[:, :, :], dend[:, :, :], ALU.mult)
            dve.memset(hb[:, 0, :], 0.0)
            dve.memset(hf[0][:, :], 0.0)

        @block.scalar
        def _(act):
            act.wait_ge(step, 2)
            act.activation(tmp3[:, :, :], tmp2[:, :, :], ACT.Exp, scale=-1.0).then_inc(acted, 1)
            act.wait_ge(step, 3)
            act.activation(cdec[:, :, :], tmp2[:, :, :], ACT.Ln).then_inc(acted, 1)
            act.activation(av[:, :], pl.prm[:, ALOG:ALOG + 2 * CH], ACT.Exp).then_inc(acted, 1)
            act.wait_ge(summed, 5)
            for j, (dst, cols) in enumerate(((dend, FW), (dend, BW), (eac, FW), (eac, BW),
                                             (cdec, slice(0, 2 * CH)))):
                src = pl.bank(j, TT * 2 * CH).rearrange("p (t h) -> p t h", t=TT)
                act.activation(dst[:, :, cols], src[:, :, cols], ACT.Exp).then_inc(acted, 1)

        @block.tensor
        def _(pe):
            pe.wait_ge(step, 10)
            rhs = dta[:, :, :].rearrange("p t h -> p (t h)")
            for j, m in enumerate((AFTER, BEFORE, UPTO, FROM, ONES)):
                pe.matmul(pl.bank(j, TT * 2 * CH), pl.c(m), rhs, start=True, stop=True).then_inc(summed, 1)

    staged1, s_full, scaled1, h_done = sem("staged1"), sem("s_full"), sem("scaled1"), sem("h_done")
    xb = pl.xb
    pairs = ((0, 1), (1, TT // 2))

    def over_pairs(eng, body):
        for lo, hi in pairs:
            if hi - lo > 1:
                with eng.Fori(lo, hi) as i:
                    for s in range(2):
                        body(i * 2 + s, s, False, i)
            else:
                for s in range(2):
                    body(s, s, True, 0)

    with nc.Block() as block:
        @block.gpsimd
        def _(pool):
            def body(o, s, first, i):
                c = (i * -2) + (TT - 1 - s)
                if not first:
                    pool.wait_ge(s_full, o - 1)
                pool.tensor_copy(b_tok1[s][:, :], xb[:, c, 512:768]).then_inc(staged1, 1)
                pool.tensor_tensor(heads(xde[s][:, :]), heads(xb[:, c, 0:512]), per_head(wde, c, BW),
                                   ALU.mult).then_inc(staged1, 1)
            over_pairs(pool, body)

        @block.tensor
        def _(pe):
            def body(o, s, first, i):
                pe.wait_ge(staged1, i * 4 + 2 * (s + 1))
                if not first:
                    pe.wait_ge(h_done, o - 1)
                for g in range(GROUPS):
                    mm = pe.matmul(pl.bank(s)[:, 256 * g:256 * (g + 1)], b_tok1[s][:, P * g:P * (g + 1)],
                                   xde[s][:, 256 * g:256 * (g + 1)], start=True, stop=True)
                mm.then_inc(s_full, 1)
            over_pairs(pe, body)

        @block.vector
        def _(dve):
            def body(o, s, first, i):
                c = (i * -2) + (TT - 1 - s)
                if not (first and s == 0):
                    dve.wait_ge(h_done, o)
                dve.tensor_tensor(heads(hb[:, o + 1, :]), heads(hb[:, o, :]), per_head(cdec, c, BW),
                                  ALU.mult).then_inc(scaled1, 1)
                dve.wait_ge(scaled1, o + 1)
                dve.wait_ge(s_full, o + 1)
                dve.tensor_tensor(hb[:, o + 1, :], hb[:, o + 1, :], pl.bank(s), ALU.add) \
                    .then_inc(h_done, 1)
            over_pairs(dve, body)

    z_in = [sem(f"z_in{s}") for s in range(2)]
    names = ("staged", "btok_in", "xfe_in", "xd_in", "skip_in", "up_in", "seg_full", "exp_done",
             "g_full", "g_done", "e_done", "st_full", "h_scaled", "hf_done", "off_full", "diag_full",
             "y1", "y2", "y3", "y4", "y5", "y_done", "sq_done")
    q = {n: sem(n) for n in names}

    with nc.Block() as block:
        def over_chunks(eng, body):
            skip = 2 if last else 0
            for lo, hi in pairs:
                if hi - lo > 1:
                    with eng.Fori(lo, hi) as i:
                        for s in range(2):
                            body(i * 2 + s, s, i * 2 + (s - 2), i * 2 + (s - skip), False, i)
                else:
                    for s in range(2):
                        body(s, s, LT + s, None if last else s, True, 0)

        @block.sync
        def _(sp):
            def body(o, s, c, y, first, i):
                if y is not None:
                    sp.wait_ge(q["y_done"], y + 1)
                    sp.dma_start(zt[s][:, :], pl.z_dram[:, c, :]).then_inc(z_in[s], 16)
            over_chunks(sp, body)

        @block.gpsimd
        def _(pool):
            def body(o, s, c, y, first, i):
                x = heads(xb[:, c, 0:512])
                if not (first and s == 0):
                    pool.wait_ge(q["st_full"], o)
                pool.tensor_copy(b_tok[:, :, :].rearrange("p g n -> p (g n)"), xb[:, c, 512:768]) \
                    .then_inc(q["btok_in"], 1)
                pool.tensor_tensor(heads(xfe[:, :]), x, per_head(wde, c, FW), ALU.mult) \
                    .then_inc(q["xfe_in"], 1)
                if y is None:
                    return
                pool.wait_ge(q["y_done"], y + 2)
                cs = lambda t: t[:, :, :].rearrange("p g (t n) -> p g t n", n=P)[:, :, c, :]
                pool.tensor_copy(b_st[:, :, :], cs(pl.bt)).then_inc(q["staged"], 1)
                pool.tensor_copy(c_st[:, :, :], cs(pl.ct)).then_inc(q["staged"], 1)
                pool.tensor_tensor(heads(xd_f[:, :]), x, per_head(dt, c, FW), ALU.mult).then_inc(q["xd_in"], 1)
                pool.tensor_tensor(heads(xd_b[:, :]), x, per_head(dt, c, BW), ALU.mult).then_inc(q["xd_in"], 1)
                skip_w = pl.prm[:, DSKIP:DSKIP + CH].unsqueeze(2).broadcast_to([P, CH, HD])
                pool.tensor_tensor(heads(xskip[:, :]), x, skip_w, ALU.mult).then_inc(q["skip_in"], 1)
            over_chunks(pool, body)

        @block.tensor
        def _(pe):
            def body(o, s, c, y, first, i):
                if y is not None:
                    pe.wait_ge(q["y_done"], y + 2)
                    for d, (m, up) in enumerate(((AFTER, up_f), (BEFORE, up_b))):
                        pe.wait_ge(q["up_in"], y * 2 + (d + 1))
                        for g in range(GROUPS):
                            mm = pe.matmul(pl.bank(2 * d + g), pl.c(m),
                                           up[:, 4 * g:4 * g + 4, :].rearrange("p h l -> p (h l)"),
                                           start=True, stop=True)
                        mm.then_inc(q["seg_full"], 1)
                    pe.wait_ge(q["staged"], y * 2 + 2)
                    pe.wait_ge(q["hf_done"], o) if not (first and s == 0) else None
                    for g in range(GROUPS):
                        mm = pe.matmul(pl.bank(4)[:, P * g:P * (g + 1)], b_st[:, g, :], c_st[:, g, :],
                                       start=True, stop=True)
                    mm.then_inc(q["g_full"], 1)
                    for d, (bank, h) in enumerate(((6, hf[s][:, :]), (7, hb[:, (c * -1) + (TT - 1), :]))):
                        for g in range(GROUPS):
                            mm = pe.matmul(pl.bank(bank)[:, 256 * g:256 * (g + 1)], c_st[:, g, :],
                                           h[:, 256 * g:256 * (g + 1)], start=True, stop=True)
                        mm.then_inc(q["off_full"], 1)
                    pe.wait_ge(q["g_done"], y * 2 + 2)
                elif not (first and s == 0):
                    pe.wait_ge(q["hf_done"], o)
                pe.wait_ge(q["btok_in"], o + 1)
                pe.wait_ge(q["xfe_in"], o + 1)
                for g in range(GROUPS):
                    mm = pe.matmul(pl.bank(4)[:, 256 * g:256 * (g + 1)], b_tok[:, g, :],
                                   xfe[:, 256 * g:256 * (g + 1)], start=True, stop=True)
                mm.then_inc(q["st_full"], 1)
                if y is not None:
                    pe.wait_ge(q["e_done"], y * 2 + 2)
                    pe.wait_ge(q["xd_in"], y * 2 + 2)
                    for h in range(CH):
                        out = pl.bank(5)[:, HD * h:HD * (h + 1)]
                        pe.matmul(out, e_f[:, h, :], xd_f[:, HD * h:HD * (h + 1)], start=True, stop=False)
                        mm = pe.matmul(out, e_b[:, h, :], xd_b[:, HD * h:HD * (h + 1)], start=False,
                                       stop=True)
                    mm.then_inc(q["diag_full"], 1)
            over_chunks(pe, body)

        @block.scalar
        def _(act):
            def body(o, s, c, y, first, i):
                if y is None:
                    return
                for d, e in enumerate((e_f, e_b)):
                    act.wait_ge(q["seg_full"], y * 2 + (d + 1))
                    act.activation(e[:, :, :].rearrange("p h l -> p (h l)"),
                                   pl.ps[:, 1024 * d:1024 * (d + 1)], ACT.Exp).then_inc(q["exp_done"], 1)
                act.wait_ge(q["y_done"], y + 3)
                for g in range(GROUPS):
                    act.activation(sq[:, 256 * g:256 * (g + 1)], pl.mixc[:, c, 256 * g:256 * (g + 1)],
                                   ACT.Square, accum_out=pl.ssq[:, c, g:g + 1]).then_inc(q["sq_done"], 1)
            over_chunks(act, body)

        @block.vector
        def _(dve):
            dve.sem_inc(q["y_done"], 2)

            def body(o, s, c, y, first, i):
                if y is not None:
                    for d, (m, up, cols) in enumerate(((UPTO, up_f, FW), (FROM, up_b, BW))):
                        dve.tensor_tensor(up[:, :, :], pl.c(m).unsqueeze(1).broadcast_to([P, CH, P]),
                                          dta[:, c, cols].unsqueeze(2).broadcast_to([P, CH, P]),
                                          ALU.mult).then_inc(q["up_in"], 1)
                    dve.wait_ge(q["g_full"], y + 1)
                    gp = pl.bank(4, 256).rearrange("p (g l) -> p g l", g=GROUPS)
                    for m, g in ((UPTO, g_f), (FROM, g_b)):
                        dve.tensor_tensor(g[:, :, :], gp, pl.c(m).unsqueeze(1).broadcast_to([P, GROUPS, P]),
                                          ALU.mult).then_inc(q["g_done"], 1)
                dve.tensor_tensor(heads(hf[1 - s][:, :]), heads(hf[s][:, :]), per_head(cdec, c, FW),
                                  ALU.mult).then_inc(q["h_scaled"], 1)
                if y is not None:
                    dve.wait_ge(q["g_done"], y * 2 + 2)
                    for d, (e, g) in enumerate(((e_f, g_f), (e_b, g_b))):
                        dve.wait_ge(q["exp_done"], y * 2 + (d + 1))
                        for k in range(GROUPS):
                            ins = dve.tensor_tensor(e[:, 4 * k:4 * k + 4, :], e[:, 4 * k:4 * k + 4, :],
                                                    g[:, k, :].unsqueeze(1).broadcast_to([P, 4, P]), ALU.mult)
                        ins.then_inc(q["e_done"], 1)
                dve.wait_ge(q["h_scaled"], o + 1)
                dve.wait_ge(q["st_full"], o + 1)
                dve.tensor_tensor(hf[1 - s][:, :], hf[1 - s][:, :], pl.bank(4), ALU.add) \
                    .then_inc(q["hf_done"], 1)
                dve.wait_ge(q["hf_done"], o + 1)
                if y is None:
                    return
                dve.wait_ge(q["off_full"], y * 2 + 2)
                dve.tensor_tensor(heads(t1[:, :]), heads(pl.bank(6)), per_head(eac, c, FW), ALU.mult) \
                    .then_inc(q["y1"], 1)
                dve.tensor_tensor(heads(t2[:, :]), heads(pl.bank(7)), per_head(eac, c, BW), ALU.mult) \
                    .then_inc(q["y2"], 1)
                dve.wait_ge(q["y1"], y + 1)
                dve.wait_ge(q["y2"], y + 1)
                dve.tensor_tensor(t1[:, :], t1[:, :], t2[:, :], ALU.add).then_inc(q["y3"], 1)
                dve.wait_ge(q["y3"], y + 1)
                dve.wait_ge(q["skip_in"], y + 1)
                dve.tensor_tensor(t1[:, :], t1[:, :], xskip[:, :], ALU.add).then_inc(q["y4"], 1)
                dve.wait_ge(q["y4"], y + 1)
                dve.wait_ge(q["diag_full"], y + 1)
                dve.tensor_tensor(t1[:, :], t1[:, :], pl.bank(5), ALU.add).then_inc(q["y5"], 1)
                dve.wait_ge(q["y5"], y + 1)
                dve.wait_ge(z_in[s], (i - (1 if last else 0)) * 16 + 16)
                dve.tensor_tensor(pl.mixc[:, c, :], t1[:, :], zt[s][:, :], ALU.mult).then_inc(q["y_done"], 1)
            over_chunks(dve, body)



def gather_mix(pl, l, last):
    nc = pl.nc
    tag = f"gm{l}"
    tiles = LT if last else TT
    chunks = (0, 1) if last else (0, 1, 2)
    width = SEQ if last else TOK
    rs = pl.at(f"{tag}_rs", [P, 2, TT, GROUPS], F32, kb=181)
    rooted, inverted, normed, x_in, turned, rounded, rest = (
        pl.sem(f"{tag}_{x}") for x in ("rooted", "inverted", "normed", "x_in", "turned", "rounded", "rest"))
    items = [(k, c) for k in range(KT) for c in chunks]
    with nc.Block() as block:
        @block.sync
        def _(sp):
            sp.dma_start(pl.x[:, :, 0:width], pl.x_dram[:, :, 0:width]).then_inc(x_in, 16)

        @block.gpsimd
        def _(pool):
            pool.wait_ge(x_in, 16)
            for k in range(KT):
                pool.tensor_scalar(pl.x[:, k, 0:width], pl.x[:, k, 0:width], ALPHA, None, ALU.mult)

        @block.scalar
        def _(act):
            act.activation(rs[:, 0, 0:tiles, :], pl.ssq[:, 0:tiles, :], ACT.Sqrt, scale=1.0 / 256.0,
                           bias=pl.small[:, 0:1]).then_inc(rooted, 1)
            for n, (k, c) in enumerate(items):
                t0, tn = CHUNKS[c]
                act.wait_ge(turned, n + 1)
                act.activation(pl.hi[:, k, t0:t0 + tn], pl.bank(n % 8, tn), ACT.Copy).then_inc(rounded, 1)

        @block.tensor
        def _(pe):
            for n, (k, c) in enumerate(items):
                t0, tn = CHUNKS[c]
                if k == 4 and c == 0:
                    pe.wait_ge(normed, tiles * GROUPS)
                if n >= 8:
                    pe.wait_ge(rest, n - 7)
                src = pl.mixab if k < 4 else pl.mixc
                for t in range(tn // P):
                    tr = pe.transpose(pl.bank(n % 8)[:, t * P:(t + 1) * P],
                                      src[:, t0 // P + t, (k % 4) * P:(k % 4 + 1) * P], pl.c(IDENT))
                tr.then_inc(turned, 1)

        @block.vector
        def _(dve):
            dve.wait_ge(rooted, 1)
            dve.reciprocal(rs[:, 1, 0:tiles, :], rs[:, 0, 0:tiles, :]).then_inc(inverted, 1)
            dve.wait_ge(inverted, 1)
            for t in range(tiles):
                for g in range(GROUPS):
                    m = pl.mixc[:, t, 256 * g:256 * (g + 1)]
                    dve.scalar_tensor_tensor(out=m, in0=m, scalar=rs[:, 1, t, g:g + 1],
                                             in1=pl.prm[:, GNORM + 256 * g:GNORM + 256 * (g + 1)],
                                             op0=ALU.mult, op1=ALU.mult).then_inc(normed, 1)
            for n, (k, c) in enumerate(items):
                t0, tn = CHUNKS[c]
                dve.wait_ge(rounded, n + 1)
                dve.tensor_tensor(pl.lo[:, k, t0:t0 + tn], pl.bank(n % 8, tn),
                                  raw(pl.hi[:, k, t0:t0 + tn]), ALU.subtract).then_inc(rest, 1)



def project_out(pl, l, last):
    nc, a = pl.nc, pl.a
    tag = f"o{l}"
    chunks = [c for c in ORDER if not (last and c == 2)]
    chunks_of = lambda kind: chunks
    segments = [(4, ["o", "o"])]
    ring = Ring(pl, tag)
    full = [pl.sem(f"{tag}_full{c}") for c in range(3)]
    taken = [pl.sem(f"{tag}_taken{c}") for c in range(3)]
    with nc.Block() as block:
        @block.sync
        def _(sp):
            over(sp, segments, chunks_of, lambda at: ring.load(sp, at, a["w_out"][l, at.n]))

        @block.gpsimd
        def _(pool):
            pool.sem_inc(ring.ready, 2)
            over(pool, segments, chunks_of, lambda at: ring.split(pool, at, full[1]))

        @block.tensor
        def _(pe):
            pe.sem_inc(full[1], 2)
            over(pe, segments, chunks_of,
                 lambda at: multiply_block(pl, pe, ring, at, chunks, full, taken))

        @block.vector
        def _(dve):
            for c in range(3):
                dve.sem_inc(taken[c], 2)

            def body(at):
                for c in chunks:
                    t0, tn = CHUNKS[c]
                    wait_full(dve, full, at, c)
                    who = 1 if c == 2 else 0
                    x = pl.x[:, at.n, t0:t0 + tn]
                    dve.scalar_tensor_tensor(out=x, in0=pl.bank(3 * at.par + c, tn),
                                             scalar=pl.mod[:, at.n + G1, who:who + 1], in1=x,
                                             op0=ALU.mult, op1=ALU.add).then_inc(taken[c], 1)
            over(dve, segments, chunks_of, body)



def layer_norm(pl, l, which, gcol, bcol, last):
    nc = pl.nc
    tag = f"ln{l}{which}"
    chunks = (0, 1) if last else (0, 1, 2)
    sq = [pl.at(f"{tag}_sq{s}", [P, 512], F32, kb=150 + 2 * s) for s in range(4)]
    sd = [pl.at(f"{tag}_sd{s}", [P, 512], F32, kb=158 + 2 * s) for s in range(2)]
    ri = [pl.at(f"{tag}_ri{s}", [P, 512], F32, kb=162 + 2 * s) for s in range(2)]
    mean_full, centred, squared, var_part, rooted, inverted, scaled = (
        pl.sem(f"{tag}_{x}") for x in ("mean_full", "centred", "squared", "var_part", "rooted",
                                       "inverted", "scaled"))
    with nc.Block() as block:
        @block.tensor
        def _(pe):
            def mean(n):
                t0, tn = CHUNKS[chunks[n]]
                for k in range(KT):
                    mm = pe.matmul(pl.bank(n, tn), pl.c(MEAN), pl.x[:, k, t0:t0 + tn], start=(k == 0),
                                   stop=(k == KT - 1))
                mm.then_inc(mean_full, 1)

            mean(0)
            for n, c in enumerate(chunks):
                if n + 1 < len(chunks):
                    mean(n + 1)
                tn = CHUNKS[c][1]
                for k in range(KT):
                    pe.wait_ge(squared, n * KT + k + 1)
                    pe.matmul(pl.bank(4 + n, tn), pl.c(MEAN), sq[k % 4][:, 0:tn], start=(k == 0),
                              stop=(k == KT - 1)).then_inc(var_part, 1)

        @block.scalar
        def _(act):
            for n, c in enumerate(chunks):
                t0, tn = CHUNKS[c]
                for k in range(KT):
                    m = n * KT + k
                    act.wait_ge(centred, m + 1)
                    if m >= 4:
                        act.wait_ge(var_part, m - 3)
                    act.activation(sq[k % 4][:, 0:tn], pl.x[:, k, t0:t0 + tn], ACT.Square) \
                        .then_inc(squared, 1)
                act.wait_ge(var_part, (n + 1) * KT)
                if n >= 2:
                    act.wait_ge(inverted, n - 1)
                act.activation(sd[n % 2][:, 0:tn], pl.bank(4 + n, tn), ACT.Sqrt,
                               bias=pl.small[:, 1:2]).then_inc(rooted, 1)

        @block.vector
        def _(dve):
            def centre(n):
                t0, tn = CHUNKS[chunks[n]]
                dve.wait_ge(mean_full, n + 1)
                for k in range(KT):
                    x = pl.x[:, k, t0:t0 + tn]
                    dve.tensor_tensor(x, x, pl.bank(n, tn), ALU.subtract).then_inc(centred, 1)

            centre(0)
            for n, c in enumerate(chunks):
                t0, tn = CHUNKS[c]
                if n + 1 < len(chunks):
                    centre(n + 1)
                dve.wait_ge(rooted, n + 1)
                dve.reciprocal(ri[n % 2][:, 0:tn], sd[n % 2][:, 0:tn]).then_inc(inverted, 1)
                dve.wait_ge(inverted, n + 1)
                for k in range(KT):
                    x = pl.x[:, k, t0:t0 + tn]
                    dve.scalar_tensor_tensor(out=x, in0=x, scalar=pl.prm[:, gcol + k:gcol + k + 1],
                                             in1=ri[n % 2][:, 0:tn], op0=ALU.mult, op1=ALU.mult) \
                        .then_inc(scaled, 1)

        @block.gpsimd
        def _(pool):
            for n, c in enumerate(chunks):
                t0, tn = CHUNKS[c]
                for k in range(KT):
                    pool.wait_ge(scaled, n * KT + k + 1)
                    x = pl.x[:, k, t0:t0 + tn]
                    pool.tensor_scalar(x, x, pl.prm[:, bcol + k:bcol + k + 1], None, ALU.add)



def feed_forward(pl, l, last):
    nc, a = pl.nc, pl.a
    tag = f"f{l}"
    chunks = [c for c in ORDER if not (last and c == 2)]
    width = SEQ if last else TOK
    n_iter = FT // 2
    kinds = ["g", "u", "g", "u", "d", "d"]
    slot = [0, 1, 2, 0, 1, 2]
    n_down = KT * len(chunks)
    act_hi = pl.at(f"{tag}_ahi", [P, 2, TOK], F32R, kb=120)
    act_lo = pl.at(f"{tag}_alo", [P, 2, TOK], F32R, kb=130)
    gated = [pl.at(f"{tag}_gated{s}", [P, TOK], F32, kb=140 + 5 * s) for s in range(2)]
    wraw = [pl.at(f"{tag}_wraw{s}", [P, D], F32, kb=150 + 4 * s) for s in range(2)]
    w_hi = [pl.at(f"{tag}_whi{s}", [P, D], F32R, kb=158 + 4 * s) for s in range(3)]
    w_lo = [pl.at(f"{tag}_wlo{s}", [P, D], F32R, kb=170 + 4 * s) for s in range(3)]

    def sem(name):
        return pl.sem(f"{tag}_{name}")
    loaded = [sem(f"loaded{s}") for s in range(2)]
    rounded, ready = sem("rounded"), sem("ready")
    gu_full = {c: sem(f"gu_full{c}") for c in chunks}
    g_taken = {c: sem(f"g_taken{c}") for c in chunks}
    u_taken = {c: sem(f"u_taken{c}") for c in chunks}
    act_hi_in = {c: sem(f"act_hi_in{c}") for c in chunks}
    act_in = {c: sem(f"act_in{c}") for c in chunks}
    down_full, down_taken = sem("down_full"), sem("down_taken")
    prescaled = sem("prescaled")

    with nc.Block() as block:
        @block.sync
        def _(sp):
            with sp.Fori(0, n_iter) as i:
                for j in range(6):
                    sp.wait_ge(ready, i * 6 + (j + 1))
                    sp.dma_start(wraw[j % 2][:, :], a["w_ffn"][l, i, j]).then_inc(loaded[j % 2], 16)

        @block.gpsimd
        def _(pool):
            pool.sem_inc(ready, 2)
            one = pl.small[:, 2:3].broadcast_to([P, D])

            def split(i, j):
                pool.wait_ge(loaded[j % 2], i * 48 + 16 * (j // 2 + 1))
                if j in (1, 2):
                    pool.wait_ge(down_full, i * n_down + 1)
                else:
                    pool.wait_ge(gu_full[1], i * 4 + {0: 1, 3: 2, 4: 3, 5: 4}[j])
                hi, lo = w_hi[slot[j]][:, :], w_lo[slot[j]][:, :]
                pool.tensor_tensor(hi, wraw[j % 2][:, :], one, ALU.mult).then_inc(rounded, 1)
                pool.wait_ge(rounded, i * 6 + (j + 1))
                pool.tensor_tensor(lo, wraw[j % 2][:, :], raw(hi), ALU.subtract).then_inc(ready, 1)

            def act_rest(i, f):
                for c in chunks:
                    t0, tn = CHUNKS[c]
                    pool.wait_ge(act_hi_in[c], i * 2 + (f + 1))
                    pool.tensor_tensor(act_lo[:, f, t0:t0 + tn], gated[f][:, t0:t0 + tn],
                                       raw(act_hi[:, f, t0:t0 + tn]), ALU.subtract).then_inc(act_in[c], 1)
            with pool.Fori(0, n_iter) as i:
                for j in range(4):
                    split(i, j)
                act_rest(i, 0)
                split(i, 4)
                split(i, 5)
                act_rest(i, 1)

        @block.tensor
        def _(pe):
            pe.sem_inc(gu_full[1], 1)
            pe.sem_inc(down_full, 1)
            with pe.Fori(0, n_iter) as i:
                for j in range(4):
                    f, up = j // 2, j % 2
                    hi = w_hi[slot[j]][:, :].rearrange("p (k n) -> p k n", n=P)
                    lo = w_lo[slot[j]][:, :].rearrange("p (k n) -> p k n", n=P)
                    pe.wait_ge(ready, i * 6 + (j + 3))
                    for c in chunks:
                        t0, tn = CHUNKS[c]
                        pe.wait_ge((u_taken if up else g_taken)[c], i * 2 + (f + 1))
                        for k in range(KT):
                            mm = three_pass(pe, pl.bank(3 * up + c, tn), hi[:, k, :], lo[:, k, :],
                                            pl.hi[:, k, t0:t0 + tn], pl.lo[:, k, t0:t0 + tn],
                                            k == 0, k == KT - 1)
                        mm.then_inc(gu_full[c], 1)
                pe.wait_ge(ready, i * 6 + 8)
                d = 0
                for c in chunks:
                    t0, tn = CHUNKS[c]
                    pe.wait_ge(act_in[c], i * 2 + 2)
                    for n in range(KT):
                        pe.wait_ge(down_taken, i * n_down + (d + 1))
                        for f in range(2):
                            cols = slice(n * P, (n + 1) * P)
                            mm = three_pass(pe, pl.bank(6 + d % 2, tn), w_hi[1 + f][:, cols],
                                            w_lo[1 + f][:, cols], act_hi[:, f, t0:t0 + tn],
                                            act_lo[:, f, t0:t0 + tn], f == 0, f == 1)
                        mm.then_inc(down_full, 1)
                        d += 1

        @block.scalar
        def _(act):
            for c in chunks:
                act.sem_inc(g_taken[c], 1)
            with act.Fori(0, n_iter) as i:
                for f in range(2):
                    for c in chunks:
                        t0, tn = CHUNKS[c]
                        act.wait_ge(gu_full[c], i * 4 + (2 * f + (2 if c == 1 else 1)))
                        act.activation(gated[f][:, t0:t0 + tn], pl.bank(c, tn), ACT.Silu) \
                            .then_inc(g_taken[c], 1)
                    for c in chunks:
                        t0, tn = CHUNKS[c]
                        act.wait_ge(u_taken[c], i * 2 + (f + 2))
                        act.activation(act_hi[:, f, t0:t0 + tn], gated[f][:, t0:t0 + tn], ACT.Copy) \
                            .then_inc(act_hi_in[c], 1)

        @block.vector
        def _(dve):
            for c in chunks:
                dve.sem_inc(u_taken[c], 1)
            dve.sem_inc(down_taken, 2)
            for k in range(KT):
                dve.tensor_scalar(pl.x[:, k, 0:width], pl.x[:, k, 0:width], ALPHA, None, ALU.mult) \
                    .then_inc(prescaled, 1)
            dve.wait_ge(prescaled, KT)
            with dve.Fori(0, n_iter) as i:
                for f in range(2):
                    for c in chunks:
                        t0, tn = CHUNKS[c]
                        dve.wait_ge(gu_full[c], i * 4 + (2 * f + (3 if c == 1 else 2)))
                        dve.wait_ge(g_taken[c], i * 2 + (f + 2))
                        g = gated[f][:, t0:t0 + tn]
                        dve.tensor_tensor(g, g, pl.bank(3 + c, tn), ALU.mult).then_inc(u_taken[c], 1)
                d = 0
                for c in chunks:
                    t0, tn = CHUNKS[c]
                    who = 1 if c == 2 else 0
                    for n in range(KT):
                        dve.wait_ge(down_full, i * n_down + (d + 2))
                        x = pl.x[:, n, t0:t0 + tn]
                        dve.scalar_tensor_tensor(out=x, in0=pl.bank(6 + d % 2, tn),
                                                 scalar=pl.mod[:, G2 + n, who:who + 1], in1=x,
                                                 op0=ALU.mult, op1=ALU.add).then_inc(down_taken, 1)
                        d += 1


def store_output(pl):
    nc = pl.nc
    stored = pl.sem("stored")
    with nc.Block() as block:
        @block.sync
        def _(sp):
            sp.dma_start(pl.a["out"], pl.x[:, :, 0:SEQ]).then_inc(stored, 16)
            sp.wait_ge(stored, 16)


def build(nc, arrays, stop=None):
    with ExitStack() as ctx:
        pl = Plan(nc, ctx, arrays)
        pl.xb = pl.at("xb_tok", [P, TT, 768], F32, kb=80)
        pl.bt = pl.at("b_feat", [P, GROUPS, TOK], F32, kb=110)
        pl.ct = pl.at("c_feat", [P, GROUPS, TOK], F32, kb=140)
        load_inputs(pl)
        pl.end_stage()
        for l in range(DEPTH):
            last = l == DEPTH - 1
            stages = [
                ("ada", lambda: modulation(pl, l)),
                ("mod1", lambda: modulate(pl, l, 1, SC1, SH1, (0, 1, 2), True)),
                ("ab", lambda: project_attention(pl, l, last)),
                ("rope", lambda: norm_and_rotate(pl, l, last)),
                ("attn", lambda: attend(pl, l, last)),
                ("c", lambda: project_ssd(pl, l, last)),
                ("ssd", lambda: scan(pl, l, last)),
                ("mix", lambda: gather_mix(pl, l, last)),
                ("out", lambda: project_out(pl, l, last)),
                ("ln1", lambda: layer_norm(pl, l, 1, LN1G, LN1B, last)),
                ("mod2", lambda: modulate(pl, l, 2, SC2, SH2, (0, 1) if last else (0, 1, 2), False)),
                ("ffn", lambda: feed_forward(pl, l, last)),
                ("ln2", lambda: layer_norm(pl, l, 2, LN2G, LN2B, last)),
            ]
            for name, stage in stages:
                stage()
                pl.end_stage()
                if stop == (l, name):
                    return pl
        store_output(pl)
    return pl



def lay_out(x, c, ctx, c_ctx, w_ada, b_ada, w_in, sink, q_gain, k_gain, conv_w, conv_b, a_log, dt_bias,
            d_skip, gnorm_w, w_out, ln1_g, ln1_b, ln2_g, ln2_b, w_gu, w_down):
    f = np.ascontiguousarray

    def feature_major(t):
        return t.T.reshape(KT, P, t.shape[0]).transpose(1, 0, 2)

    def columns(v):
        return v.reshape(DEPTH, -1, P).transpose(0, 2, 1)

    def rows(v):
        return np.broadcast_to(v.reshape(DEPTH, 1, -1), (DEPTH, P, v.size // DEPTH))

    def blocks(w, n):
        return w.reshape(DEPTH, w.shape[1] // P, P, -1, n).transpose(0, 3, 2, 1, 4)

    order = []
    for base in (0, 512):
        for heads in ((0, 2), (1, 3)):
            for h in heads:
                order += list(range(base + HD * h, base + HD * (h + 1)))
        order += list(range(base + 256, base + 512))
    order += list(range(1024, 2560)) + list(range(2576 - P, 2576))
    w_gate, w_up = blocks(w_gu[:, :, :D_FF], P), blocks(w_gu[:, :, D_FF:], P)
    down = w_down.reshape(DEPTH, FT, P, KT, P)
    w_ffn = np.stack([w_gate[:, 0::2], w_up[:, 0::2], w_gate[:, 1::2], w_up[:, 1::2],
                      down[:, 0::2], down[:, 1::2]], 2)
    conv = conv_w.transpose(0, 2, 1).reshape(DEPTH, 8, P, CONV).transpose(0, 2, 1, 3)
    gain = lambda g: np.concatenate([g, g], 1)[:, :, None]
    prm = np.concatenate([columns(ln1_g), columns(ln1_b), columns(ln2_g), columns(ln2_b), columns(b_ada),
                          conv.reshape(DEPTH, P, 8 * CONV), columns(conv_b), gain(q_gain), gain(k_gain),
                          rows(sink), rows(dt_bias), rows(a_log), rows(d_skip), rows(gnorm_w)], 2)
    cT = np.stack([c[0], c_ctx], 1).reshape(KT, P, 2).transpose(1, 0, 2)
    xT = np.concatenate([feature_major(x[0]), feature_major(ctx[0])], 2)
    return {
        "consts": const_table(), "rope": rope_table(), "cT": f(cT), "xT": f(xT), "prm": f(prm),
        "w_ada": f(blocks(w_ada, 4 * P)), "w_in": f(blocks(w_in[:, :, order], P).reshape(DEPTH, 21, P, D)),
        "w_out": f(blocks(w_out, P).reshape(DEPTH, KT, P, D)),
        "w_ffn": f(w_ffn.reshape(DEPTH, FT // 2, 6, P, D)),
    }


def kernel(**inputs):
    import concourse.bacc as bacc
    from concourse.bass_utils import run_bass_kernel_spmd

    nc = bacc.Bacc("TRN2", target_bir_lowering=False, num_devices=1)
    data = lay_out(**{k: np.asarray(v) for k, v in inputs.items()})
    arrays = {k: nc.dram_tensor(f"in_{k}", v.shape, F32, kind="ExternalInput").ap() for k, v in data.items()}
    arrays["out"] = nc.dram_tensor("out_x", (P, KT, SEQ), F32, kind="ExternalOutput").ap()
    build(nc, arrays)
    r = run_bass_kernel_spmd(nc, [{f"in_{k}": v for k, v in data.items()}], core_ids=[0])
    y = r.results[0]["out_x"]
    return np.ascontiguousarray(y.transpose(1, 0, 2).reshape(D, SEQ).T)[None]
```

```python
from contextlib import ExitStack

import numpy as np

import concourse.bass as bass
from concourse import mybir

ALU = mybir.AluOpType
ACT = mybir.ActivationFunctionType
AX = mybir.AxisListType
F32 = mybir.dt.float32
F32R = mybir.dt.float32r

P = 128
D = 1024
SEQ = 1024
CTX = 256
TOK = SEQ + CTX
DEPTH = 2
GRID_W = 64
HD = 64
HEADS = 4
CH = 8
GROUPS = 2
CONV = 5
D_FF = 2816
KT = D // P
TT = TOK // P
LT = SEQ // P
FT = D_FF // P
SCALE = float(HD) ** -0.5
ALPHA = float((2 * DEPTH) ** 0.25)
LN_EPS = 1e-5
RMS_EPS = 1e-6
NEG = -1.0e30

CHUNKS = ((0, 512), (512, 512), (SEQ, CTX))
ORDER = (2, 0, 1)

IDENT, UPTO, FROM, AFTER, BEFORE, ONES, MEAN, BLOCK64, ROT, MASKS = (P * j for j in range(10))
N_CONST = MASKS + 3 * 3 * P

LN1G, LN1B, LN2G, LN2B = 0, 8, 16, 24
CONVW = 32
CONVB = CONVW + 8 * CONV
QGAIN = CONVB + 8
KGAIN = QGAIN + 1
SINK = KGAIN + 1
DTB = SINK + HEADS
ALOG = DTB + 2 * CH
DSKIP = ALOG + 2 * CH
GNORM = DSKIP + CH
N_PRM = GNORM + 4

SH1, SC1, G1, SH2, SC2, G2 = (KT * j for j in range(6))


def const_table():
    t = np.zeros((P, N_CONST), np.float32)
    r, c = np.arange(P)[:, None], np.arange(P)[None, :]
    t[:, IDENT:IDENT + P] = r == c
    t[:, UPTO:UPTO + P] = r <= c
    t[:, FROM:FROM + P] = r >= c
    t[:, AFTER:AFTER + P] = r > c
    t[:, BEFORE:BEFORE + P] = r < c
    t[:, ONES:ONES + P] = 1.0
    t[:, MEAN:MEAN + P] = 1.0 / D
    t[:, BLOCK64:BLOCK64 + P] = (r // HD == c // HD) / float(HD)
    quarter = HD // 4
    first, second = (r // quarter) % 2 == 0, (r // quarter) % 2 == 1
    t[:, ROT:ROT + P] = 1.0 * (first & (c == r + quarter)) - 1.0 * (second & (c == r - quarter))
    left = np.where(c >= r, 0.0, NEG)
    right = np.where(c <= r, 0.0, NEG)
    free, shut = np.zeros((P, P)), np.full((P, P), NEG)
    for v, parts in enumerate(((shut, free, right), (left, free, right), (left, free, shut))):
        t[:, MASKS + 3 * P * v:MASKS + 3 * P * (v + 1)] = np.concatenate(parts, 1)
    return t


def rope_table():
    n = np.arange(SEQ)
    freqs = HD // 4
    inv = np.float32(10000.0) ** (-np.arange(freqs, dtype=np.float32) / np.float32(freqs))
    ang = np.stack([n // GRID_W, n % GRID_W], -1).astype(np.float32)[..., None] * inv
    ang = np.broadcast_to(ang.transpose(1, 2, 0)[None, :, None], (2, 2, 2, freqs, SEQ)).reshape(P, SEQ)
    return np.stack([np.cos(ang), np.sin(ang)], 1).astype(np.float32)


class Plan:

    def __init__(self, nc, ctx, arrays):
        self.nc, self.ctx, self.a = nc, ctx, arrays
        self.stage_sems = []
        self.base = 16512
        self.top = self.base + 27 * 512
        at = self.at
        self.const = at("const", [P, N_CONST], F32, low=0)
        self.prm = at("prm", [P, N_PRM], F32, low=9216)
        self.mod = at("mod", [P, 48, 2], F32, low=12032)
        self.dtr = at("dtr", [P, TT, 2 * CH], F32, low=12544)
        self.small = at("small", [P, 32], F32, low=13312)
        self.ssq = at("ssq", [P, TT, GROUPS], F32, low=13440)
        self.bada = at("b_ada", [P, 48], F32, low=13568)
        self.hi = at("h_hi", [P, KT, TOK], F32R, kb=0)
        self.lo = at("h_lo", [P, KT, TOK], F32R, kb=40)
        self.hi_f32 = at("h_hi_f32", [P, KT, TOK], F32, kb=0)
        self.lo_f32 = at("h_lo_f32", [P, KT, TOK], F32, kb=40)
        self.x = at("x_res", [P, KT, TOK], F32, kb=80)
        self.qk = at("qk", [P, 6, TOK], F32, kb=80)
        self.v = at("v_tok", [P, TT, 256], F32, kb=110)
        self.mixab = at("mix_ab", [P, TT, 512], F32, kb=120)
        self.mixc = at("mix_c", [P, TT, 512], F32, kb=150)
        self.ps = ctx.enter_context(nc.psum_tensor("ps", [P, 8 * 512], F32))
        self.x_dram = nc.dram_tensor("x_spill", [P, KT, TOK], F32, kind="Internal").ap()
        self.z_dram = nc.dram_tensor("z_spill", [P, TT, 512], F32, kind="Internal").ap()

    def at(self, name, shape, dtype, kb=None, low=None):
        off = self.base + low if kb is None else self.top + int(kb * 1024)
        return self.nc.alloc_sbuf_tensor_at(name, shape, dtype, offset=off)

    def sem(self, name):
        self.stage_sems.append(self.nc.alloc_semaphore(name))
        return self.stage_sems[-1]

    def end_stage(self):
        self.nc.clear_and_free_semaphores(self.stage_sems)
        self.nc.all_engine_barrier()
        self.stage_sems = []

    def c(self, col, n=P):
        return self.const[:, col:col + n]

    def bank(self, b, n=512):
        return self.ps[:, 512 * b:512 * b + n]


class Lead:

    def __init__(self, ready, tensor, scalar, vector, gpsimd=None, sync=None, prm_free=None):
        self.ready, self.prm_free = ready, prm_free
        self.tensor, self.scalar, self.vector = tensor, scalar, vector
        self.gpsimd = gpsimd or (lambda pool: None)
        self.sync = sync or (lambda sp: None)


def raw(t):
    return t.bitcast(F32)


def three_pass(pe, out, w_hi, w_lo, h_hi, h_lo, first, last):
    pe.matmul(out, w_hi, h_hi, start=first, stop=False)
    pe.matmul(out, w_hi, h_lo, start=False, stop=False)
    return pe.matmul(out, w_lo, h_hi, start=False, stop=last)


class At:

    def __init__(self, n, par, kind, i, j, half, m2):
        self.n, self.par, self.kind, self.i, self.j, self.half, self.m2 = n, par, kind, i, j, half, m2

    def number(self, c):
        return self.m2 if c == 2 else self.n


def over(eng, segments, chunks_of, body, start=0):
    n0, m0 = start, 0
    for count, kinds in segments:
        with2 = [int(2 in chunks_of(k)) for k in kinds]

        def run(i):
            for j, k in enumerate(kinds):
                body(At(i * len(kinds) + (n0 + j), (n0 + j) % 2, k, i, j,
                        i * (len(kinds) // 2) + (n0 + j) // 2, i * sum(with2) + (m0 + sum(with2[:j]))))
        if count > 1:
            with eng.Fori(0, count) as i:
                run(i)
        else:
            run(0)
        n0 += count * len(kinds)
        m0 += count * sum(with2)



class Modulation:

    SLOTS = 4

    def __init__(self, pl, l, first, end, scale_tiles):
        self.pl, self.l, self.first, self.end, self.scale_tiles = pl, l, first, end, scale_tiles
        tag = f"ada{l}_{first}"
        self.w = [pl.at(f"{tag}_w{s}", [P, D], F32, kb=120 + 4 * s) for s in range(self.SLOTS)]
        self.cond = pl.at(f"{tag}_cond", [P, 2, D], F32, kb=136)
        self.product = pl.at(f"{tag}_product", [P, D], F32, kb=144)
        self.w_in = [pl.sem(f"{tag}_w_in{s}") for s in range(self.SLOTS)]
        self.cond_in, self.bias_in = pl.sem(f"{tag}_cond_in"), pl.sem(f"{tag}_bias_in")
        self.cond_ready = pl.sem(f"{tag}_cond_ready")
        self.first_done = pl.sem(f"{tag}_first_done")
        self.tile_done = pl.sem(f"{tag}_tile_done")
        self.biased = pl.sem(f"{tag}_biased")

    def start(self, sp):
        pl, a = self.pl, self.pl.a
        sp.dma_start(self.cond[:, :, :], a["cond"]).then_inc(self.cond_in, 16)
        sp.dma_start(pl.bada[:, :], a["b_ada"][self.l]).then_inc(self.bias_in, 16)
        sp.sem_inc(self.tile_done, self.SLOTS)

    def load(self, sp, r):
        n = self.SLOTS
        for s in range(n):
            sp.wait_ge(self.tile_done, r * n + (s + 1))
            sp.dma_start(self.w[s][:, :], self.pl.a["w_ada"][self.l, r * n + (s + self.first)]) \
                .then_inc(self.w_in[s], 16)

    def silu(self, act):
        act.wait_ge(self.cond_in, 16)
        act.activation(self.cond[:, :, :], self.cond[:, :, :], ACT.Silu).then_inc(self.cond_ready, 1)

    def sums(self, dve, r):
        n = self.SLOTS
        for s in range(n):
            dve.wait_ge(self.w_in[s], r * 16 + 16)
            dve.wait_ge(self.tile_done, r * n + (s + n))
            tile = r * n + (s + self.first)
            for c, done in ((0, self.first_done), (1, self.tile_done)):
                dve.scalar_tensor_tensor(out=self.product[:, :], in0=self.w[s][:, :], scalar=1.0,
                                         in1=self.cond[:, c, :], op0=ALU.mult, op1=ALU.mult,
                                         accum_out=self.pl.mod[:, tile, c:c + 1]).then_inc(done, 1)
                if c == 0:
                    dve.wait_ge(done, r * n + (s + 1))

    def finish(self, dve):
        pl, count = self.pl, self.end - self.first
        dve.wait_ge(self.bias_in, 16)
        dve.wait_ge(self.tile_done, count + self.SLOTS)
        part = pl.mod[:, self.first:self.end, :]
        bias = pl.bada[:, self.first:self.end].unsqueeze(2).broadcast_to([P, count, 2])
        dve.tensor_tensor(part, part, bias, ALU.add).then_inc(self.biased, 1)
        dve.wait_ge(self.biased, 1)
        t = self.scale_tiles
        dve.tensor_scalar(pl.mod[:, t:t + KT, :], pl.mod[:, t:t + KT, :], 1.0, None, ALU.add)


def first_modulation(pl, l):
    return Modulation(pl, l, SH1, G1, SC1)


def other_modulation(pl, l):
    return Modulation(pl, l, G1, 6 * KT, SC2)



def load_inputs(pl):
    nc, a = pl.nc, pl.a
    loaded = pl.sem("start_loaded")
    ada = first_modulation(pl, 0)
    with nc.Block() as block:
        @block.sync
        def _(sp):
            ada.start(sp)
            with sp.Fori(0, G1 // ada.SLOTS) as r:
                ada.load(sp, r)
                for j in range(2):
                    sp.dma_start(pl.x[:, r * 2 + j, :], a["xT"][:, r * 2 + j, :]).then_inc(loaded, 16)
            sp.dma_start(pl.const[:, :], a["consts"]).then_inc(loaded, 16)
            sp.wait_ge(loaded, 16 * (KT + 1))

        @block.scalar
        def _(act):
            ada.silu(act)

        @block.vector
        def _(dve):
            dve.memset(pl.small[:, 0:1], RMS_EPS)
            dve.memset(pl.small[:, 1:2], LN_EPS)
            dve.memset(pl.small[:, 2:3], 1.0)
            dve.wait_ge(ada.cond_ready, 1)
            with dve.Fori(0, G1 // ada.SLOTS) as r:
                ada.sums(dve, r)
            ada.finish(dve)



def modulate_inputs(pl):
    tmp = [pl.at(f"modt{s}", [P, TOK], F32, kb=148 + 5 * s) for s in range(3)]
    scaled, rounded, kept, spilled = (pl.sem(f"mod_{x}") for x in ("scaled", "rounded", "kept", "spilled"))
    rest = [pl.sem(f"mod_rest{s}") for s in range(2)]

    def vector(dve, between):
        def rest_of(k):
            dve.wait_ge(rounded, k + 1)
            dve.tensor_tensor(pl.lo[:, k, :], tmp[k % 3][:, :], raw(pl.hi[:, k, :]), ALU.subtract) \
                .then_inc(rest[1], 1)
        for k in range(KT):
            if k == 2:
                between()
            if k >= 3:
                dve.wait_ge(rest[(k - 3) % 2], (k - 3) // 2 + 1)
            for (t0, t1), who in (((0, SEQ), 0), ((SEQ, TOK), 1)):
                dve.tensor_scalar(tmp[k % 3][:, t0:t1], pl.x[:, k, t0:t1],
                                  pl.mod[:, SC1 + k, who:who + 1], pl.mod[:, SH1 + k, who:who + 1],
                                  ALU.mult, ALU.add).then_inc(scaled, 1)
            dve.wait_ge(scaled, 2 * k + 2)
            dve.tensor_scalar(pl.x[:, k, :], pl.x[:, k, :], ALPHA, None, ALU.mult).then_inc(kept, 1)
            if k >= 2 and k % 2 == 0:
                rest_of(k - 1)
        rest_of(KT - 1)

    def scalar(act):
        for k in range(KT):
            act.wait_ge(scaled, 2 * k + 2)
            act.activation(pl.hi[:, k, :], tmp[k % 3][:, :], ACT.Copy).then_inc(rounded, 1)
            act.wait_ge(kept, k + 1)
            act.dma_start(pl.x_dram[:, k, :], pl.x[:, k, :]).then_inc(spilled, 16)
        act.wait_ge(spilled, KT * 16)

    def gpsimd(pool):
        for k in range(0, KT, 2):
            pool.wait_ge(rounded, k + 1)
            pool.tensor_tensor(pl.lo[:, k, :], tmp[k % 3][:, :], raw(pl.hi[:, k, :]), ALU.subtract) \
                .then_inc(rest[0], 1)

    ready = {c: [(rest[0], KT // 2), (rest[1], KT // 2)] for c in range(3)}
    return Lead(ready, lambda pe: None, scalar, vector, gpsimd)



class Ring:

    def __init__(self, pl, tag, kb=167):
        self.raw = [pl.at(f"wraw{tag}{s}", [P, D], F32, kb=kb + 4 * s) for s in range(2)]
        self.hi = [pl.at(f"whi{tag}{s}", [P, KT, P], F32R, kb=kb + 8 + 4 * s) for s in range(2)]
        self.lo = [pl.at(f"wlo{tag}{s}", [P, KT, P], F32R, kb=kb + 16 + 4 * s) for s in range(2)]
        self.one = pl.small[:, 2:3].broadcast_to([P, D])
        self.loaded = [pl.sem(f"w_loaded{tag}{s}") for s in range(2)]
        self.rounded = pl.sem(f"w_rounded{tag}")
        self.ready = pl.sem(f"w_ready{tag}")

    def load(self, sp, at, src):
        sp.wait_ge(self.ready, at.n + 1)
        sp.dma_start(self.raw[at.par][:, :], src).then_inc(self.loaded[at.par], 16)

    def round_first(self, act):
        for n in range(2):
            act.wait_ge(self.loaded[n], 16)
            act.activation(self.hi[n][:, :, :].rearrange("p k n -> p (k n)"), self.raw[n][:, :],
                           ACT.Copy).then_inc(self.rounded, 1)

    def rest_first(self, dve):
        for n in range(2):
            hi, lo = (t[n][:, :, :].rearrange("p k n -> p (k n)") for t in (self.hi, self.lo))
            dve.wait_ge(self.rounded, n + 1)
            dve.tensor_tensor(lo, self.raw[n][:, :], raw(hi), ALU.subtract).then_inc(self.ready, 1)

    def split(self, pool, at, done):
        w, hi, lo = self.raw[at.par][:, :], self.hi[at.par], self.lo[at.par]
        hi, lo = (t[:, :, :].rearrange("p k n -> p (k n)") for t in (hi, lo))
        pool.wait_ge(self.loaded[at.par], at.half * 16 + 16)
        pool.wait_ge(done, at.n + 1)
        pool.tensor_tensor(hi, w, self.one, ALU.mult).then_inc(self.rounded, 1)
        pool.wait_ge(self.rounded, at.n + 1)
        pool.tensor_tensor(lo, w, raw(hi), ALU.subtract).then_inc(self.ready, 1)


def multiply_block(pl, pe, ring, at, chunks, full, taken, ready=None):
    pe.wait_ge(ring.ready, at.n + 3)
    for c in ORDER:
        if c in chunks:
            t0, tn = CHUNKS[c]
            for sem, count in ready[c] if ready is not None else ():
                pe.wait_ge(sem, count)
            pe.wait_ge(taken[c], at.number(c) + 1)
            for k in range(KT):
                mm = three_pass(pe, pl.bank(3 * at.par + c, tn), ring.hi[at.par][:, k, :],
                                ring.lo[at.par][:, k, :], pl.hi[:, k, t0:t0 + tn],
                                pl.lo[:, k, t0:t0 + tn], k == 0, k == KT - 1)
            mm.then_inc(full[c], 1)


def wait_full(eng, full, at, c):
    eng.wait_ge(full[c], at.number(c) + (3 if c == 1 else 1))


PADDED = (2, 514, SEQ + 6)


def transpose_chunk(pl, pe, src, c, bank):
    for t in range(CHUNKS[c][1] // P):
        p0 = PADDED[c] + t * P
        tr = pe.transpose(pl.bank(bank)[:, t * P:(t + 1) * P], src[:, p0:p0 + P], pl.c(IDENT))
    return tr



def project_attention(pl, l, last, lead):
    nc, a = pl.nc, pl.a
    tag = f"ab{l}"
    chunks_of = lambda kind: (0, 1) if last and kind in ("q0", "q1") else ORDER
    segments = [(2, ["q0", "q1", "k", "v"])]
    ring = Ring(pl, tag)
    full = [pl.sem(f"{tag}_full{c}") for c in range(3)]
    taken = [pl.sem(f"{tag}_taken{c}") for c in range(3)]
    vst = pl.at(f"{tag}_vst", [P, TOK + 8], F32, kb=150)
    turned = pl.sem(f"{tag}_turned")
    stored = pl.sem(f"{tag}_stored")
    prm_in = pl.sem(f"{tag}_prm_in")
    ada = other_modulation(pl, l)
    with nc.Block() as block:
        @block.sync
        def _(sp):
            load = lambda at: ring.load(sp, at, a["w_in"][l, at.n])
            over(sp, [(1, ["w", "w"])], lambda kind: (), load)
            ada.start(sp)
            if lead.prm_free is not None:
                sp.wait_ge(*lead.prm_free)
            sp.dma_start(pl.prm[:, :], a["prm"][l]).then_inc(prm_in, 16)

            def body(at):
                load(at)
                ada.load(sp, at.n - 2)
            over(sp, [(3, ["w", "w"])], lambda kind: (), body, start=2)
            for r in (6, 7):
                ada.load(sp, r)
            sp.wait_ge(prm_in, 16)

        @block.gpsimd
        def _(pool):
            pool.sem_inc(ring.ready, 2)
            lead.gpsimd(pool)
            over(pool, [(3, ["w", "w"])], lambda kind: (), lambda at: ring.split(pool, at, full[1]), start=2)

        @block.tensor
        def _(pe):
            pe.sem_inc(full[1], 2)
            lead.tensor(pe)

            def body(at):
                multiply_block(pl, pe, ring, at, chunks_of(at.kind), full, taken,
                               lead.ready)
                if at.kind == "v":
                    for g, c in enumerate(ORDER):
                        pe.wait_ge(taken[c], at.number(c) + 3)
                        pe.wait_ge(stored, at.i * 3 + (g + 1 if g < 2 else 2))
                        transpose_chunk(pl, pe, vst, c, 6 + g % 2).then_inc(turned, 1)
            over(pe, segments, chunks_of, body)

        @block.scalar
        def _(act):
            for c in range(3):
                act.sem_inc(taken[c], 2)
            ring.round_first(act)
            lead.scalar(act)
            ada.silu(act)

            def body(at):
                for c in ORDER:
                    if c not in chunks_of(at.kind):
                        continue
                    t0, tn = CHUNKS[c]
                    wait_full(act, full, at, c)
                    if at.kind == "v":
                        dst = vst[:, PADDED[c]:PADDED[c] + tn]
                    else:
                        dst = pl.qk[:, at.i * 3 + at.j, t0:t0 + tn]
                    act.activation(dst, pl.bank(3 * at.par + c, tn), ACT.Copy).then_inc(taken[c], 1)
            over(act, segments, chunks_of, body)

        @block.vector
        def _(dve):
            dve.sem_inc(stored, 1)
            lead.vector(dve, lambda: ring.rest_first(dve))
            dve.wait_ge(ada.cond_ready, 1)
            with dve.Fori(0, 2) as i:
                with dve.Fori(0, 4) as j:
                    ada.sums(dve, i * 4 + j)
                for g, c in enumerate(ORDER):
                    t0, tn = CHUNKS[c]
                    dve.wait_ge(turned, i * 3 + (g + 1))
                    tt = slice(t0 // P, (t0 + tn) // P)
                    dve.tensor_copy(pl.v[:, tt, :].rearrange("p t (g d) -> p t g d", g=2)[:, :, i, :],
                                    pl.bank(6 + g % 2, tn).rearrange("p (t d) -> p t d", d=P)) \
                        .then_inc(stored, 1)
            ada.finish(dve)



def norm_and_rotate(pl, l, last):
    nc = pl.nc
    tag = f"nr{l}"
    norms = [(t, c) for t in (3, 4, 5) for c in ORDER if not (last and t < 5 and c == 2)]
    turns = [(t, c) for t in range(6) for c in (0, 1)]
    rope = pl.at(f"{tag}_rope", [P, 2, SEQ], F32, kb=161)
    sq = [pl.at(f"{tag}_sq{s}", [P, 512], F32, kb=169 + 2 * s) for s in range(2)]
    rt = [pl.at(f"{tag}_rt{s}", [P, 512], F32, kb=173 + 2 * s) for s in range(2)]
    ri = [pl.at(f"{tag}_ri{s}", [P, 512], F32, kb=177 + 2 * s) for s in range(2)]
    xc = [pl.at(f"{tag}_xc{s}", [P, 512], F32, kb=181 + 2 * s) for s in range(2)]
    xs = [pl.at(f"{tag}_xs{s}", [P, 512], F32, kb=185 + 2 * s) for s in range(2)]
    table = pl.sem(f"{tag}_table")
    squared, summed, rooted, inverted, normed = (pl.sem(f"{tag}_{x}") for x in
                                                 ("squared", "summed", "rooted", "inverted", "normed"))
    with_cos, rotated, with_sin, done = ([pl.sem(f"{tag}_{x}{g}") for g in range(2)] for x in
                                         ("with_cos", "rotated", "with_sin", "done"))
    brought = pl.sem(f"{tag}_brought")
    N = len(norms)

    def normed_before(t):
        return sum(1 for u, _ in norms if u <= t)

    def wait_turned(eng, n):
        if n >= 0:
            eng.wait_ge(done[n // 6], n % 6 + 1)

    def turn(eng, n, t, t0, tn):
        g, m = divmod(n, 6)
        if g == 0:
            eng.wait_ge(brought, m + 1)
            source = xs[n % 2][:, :]
        else:
            eng.wait_ge(rotated[g], m + 1)
            wait_turned(eng, n - 2)
            source = pl.bank(2 + n % 2, tn)
        eng.tensor_tensor(xs[n % 2][:, :], source, rope[:, 1, t0:t0 + tn], ALU.mult) \
            .then_inc(with_sin[g], 1)
        eng.wait_ge(with_sin[g], m + 1)
        eng.wait_ge(with_cos[g], m + 1)
        eng.tensor_tensor(pl.qk[:, t, t0:t0 + tn], xc[n % 2][:, :], xs[n % 2][:, :], ALU.add) \
            .then_inc(done[g], 1)

    with nc.Block() as block:
        @block.sync
        def _(sp):
            sp.dma_start(rope[:, :, :], pl.a["rope"]).then_inc(table, 16)
            sp.wait_ge(table, 16)

        @block.scalar
        def _(act):
            def square(n):
                t, c = norms[n]
                t0, tn = CHUNKS[c]
                if n >= 2:
                    act.wait_ge(summed, n - 1)
                act.activation(sq[n % 2][:, 0:tn], pl.qk[:, t, t0:t0 + tn], ACT.Square) \
                    .then_inc(squared, 1)
            def bring(n):
                tn = CHUNKS[turns[n][1]][1]
                act.wait_ge(rotated[0], n + 1)
                wait_turned(act, n - 2)
                act.activation(xs[n % 2][:, 0:tn], pl.bank(2 + n % 2, tn), ACT.Copy).then_inc(brought, 1)

            square(0)
            for n, (t, c) in enumerate(norms):
                if n + 1 < N:
                    square(n + 1)
                tn = CHUNKS[c][1]
                act.wait_ge(summed, n + 1)
                if n >= 2:
                    act.wait_ge(inverted, n - 1)
                act.activation(rt[n % 2][:, 0:tn], pl.bank(n % 2, tn), ACT.Sqrt,
                               bias=pl.small[:, 0:1]).then_inc(rooted, 1)
                if n < 6:
                    bring(n)

        @block.tensor
        def _(pe):
            def rotate(n):
                t, c = turns[n]
                t0, tn = CHUNKS[c]
                if t >= 3:
                    pe.wait_ge(normed, normed_before(t))
                if 2 <= n < 8:
                    pe.wait_ge(brought, n - 1)
                elif n >= 8:
                    pe.wait_ge(with_sin[1], n - 7)
                pe.matmul(pl.bank(2 + n % 2, tn), pl.c(ROT), pl.qk[:, t, t0:t0 + tn], start=True,
                          stop=True).then_inc(rotated[n // 6], 1)

            for n, (t, c) in enumerate(norms):
                tn = CHUNKS[c][1]
                pe.wait_ge(squared, n + 1)
                if n >= 2:
                    pe.wait_ge(rooted, n - 1)
                pe.matmul(pl.bank(n % 2, tn), pl.c(BLOCK64), sq[n % 2][:, 0:tn], start=True,
                          stop=True).then_inc(summed, 1)
                if n < 6:
                    rotate(n)
            for n in range(6, len(turns)):
                rotate(n)

        @block.gpsimd
        def _(pool):
            pool.wait_ge(table, 16)
            for n, (t, c) in enumerate(turns):
                t0, tn = CHUNKS[c]
                if t >= 3:
                    pool.wait_ge(normed, normed_before(t))
                wait_turned(pool, n - 2)
                pool.tensor_tensor(xc[n % 2][:, :], pl.qk[:, t, t0:t0 + tn], rope[:, 0, t0:t0 + tn],
                                   ALU.mult).then_inc(with_cos[n // 6], 1)
                if t < 3:
                    turn(pool, n, t, t0, tn)

        @block.vector
        def _(dve):
            for n, (t, c) in enumerate(norms):
                t0, tn = CHUNKS[c]
                gain = pl.prm[:, (KGAIN if t == 5 else QGAIN):(KGAIN if t == 5 else QGAIN) + 1]
                dve.wait_ge(rooted, n + 1)
                dve.reciprocal(ri[n % 2][:, 0:tn], rt[n % 2][:, 0:tn]).then_inc(inverted, 1)
                dve.wait_ge(inverted, n + 1)
                x = pl.qk[:, t, t0:t0 + tn]
                dve.scalar_tensor_tensor(out=x, in0=x, scalar=gain, in1=ri[n % 2][:, 0:tn],
                                         op0=ALU.mult, op1=ALU.mult).then_inc(normed, 1)
            dve.wait_ge(table, 16)
            for n, (t, c) in enumerate(turns):
                if t >= 3:
                    turn(dve, n, t, *CHUNKS[c])



def attend(pl, l, last):
    nc = pl.nc
    tag = f"at{l}"
    tiles = LT if last else TT
    blocks = [("A" if i < LT else "C", i, 0) for i in range(tiles)] + \
             [("B" if i < LT else "C", i, 1) for i in range(tiles)]
    n_keys = {"A": 5, "B": TT, "C": 2}
    groups = {"A": ((0, 4), (4, 5)), "B": ((0, 4), (4, 8), (8, 10)), "C": ((0, 2),)}
    segments = [(0, 1), (1, 2), (2, 6), (6, 7), (7, 8)] + [(i, i + 1) for i in range(8, tiles)]
    segments += [(tiles, tiles + 1), (tiles + 1, tiles + 7), (tiles + 7, tiles + 8)]
    segments += [(i, i + 1) for i in range(tiles + 8, 2 * tiles)]
    late = [0]
    for kind, _, _ in blocks:
        late.append(late[-1] + HEADS * (len(groups[kind]) - 1))

    prob = [pl.at(f"{tag}_prob{s}", [P, TOK], F32, kb=161 + 5 * s) for s in range(2)]
    turned = [pl.at(f"{tag}_turned{s}", [P, TOK], F32, kb=171 + 5 * s) for s in range(2)]
    k_hi = pl.at(f"{tag}_k_hi", [P, 2, TOK], F32R, kb=140)
    k_lo = pl.at(f"{tag}_k_lo", [P, 6, TOK], F32R, kb=80)
    qst = pl.at(f"{tag}_qst", [P, HEADS, P], F32, kb=181)
    q_hi, q_lo = (pl.at(f"{tag}_q_{x}", [P, HEADS, P], F32R, kb=b) for x, b in (("hi", 184), ("lo", 186)))
    st = pl.at(f"{tag}_st", [P, 64], F32, kb=183)
    mx, nm, es, den, dn, rd = ([st[:, HEADS * j + h:HEADS * j + h + 1] for h in range(HEADS)]
                               for j in range(6))
    nsink = st[:, 6 * HEADS:7 * HEADS]

    s_full, masked, maxed, nm_done, p_done, es_done, dn_done, rd_done, q_ready, nsink_done = (
        pl.sem(f"{tag}_{x}") for x in ("s_full", "masked", "maxed", "nm_done", "p_done", "es_done",
                                       "dn_done", "rd_done", "q_ready", "nsink_done"))
    q_staged, q_rounded, k_rounded, k_split = (
        pl.sem(f"{tag}_{x}") for x in ("q_staged", "q_rounded", "k_rounded", "k_split"))
    t_full, first_copied, later_copied, pv_done, o_done = (
        pl.sem(f"{tag}_{x}") for x in ("t_full", "first_copied", "later_copied", "pv_done", "o_done"))

    class Unit:

        def __init__(self, r, b, h):
            self.kind, _, self.group = blocks[r]
            self.h, self.b, self.r = h, b, r
            self.i = b if self.group == 0 else b - tiles
            self.static = isinstance(b, int)
            self.u = b * HEADS + h
            self.par = h % 2
            per = len(groups[self.kind]) - 1
            self.late = (b - r) * (HEADS * per) + (late[r] + h * per)
            self.all = self.late + self.u

        def step(self, d):
            if abs(d) == 2:
                v = self.step(d // 2)
                return None if v is None else v.step(d // 2)
            h = self.h + d
            if h in range(HEADS):
                return Unit(self.r, self.b, h)
            r = self.r + (1 if d > 0 else -1)
            if r not in range(len(blocks)):
                return None
            return Unit(r, self.b + (1 if d > 0 else -1), h % HEADS)

        def keys(self):
            if self.kind == "A":
                i = self.i
                window = [max(i - 1, 0), i, min(i + 1, LT - 1)] if self.static else [i - 1, i, i + 1]
                return window + [LT, LT + 1]
            return list(range(TT)) if self.kind == "B" else [LT, LT + 1]

        def runs(self):
            k = self.keys()
            if self.kind == "B":
                return [(0, 0, 4), (4, 4, 4), (8, 8, 2)]
            if self.kind == "C":
                return [(0, LT, 2)]
            if self.static and self.i == 0:
                window = [(0, 0, 1), (1, 0, 2)]
            elif self.static and self.i == LT - 1:
                window = [(0, LT - 2, 2), (2, LT - 1, 1)]
            else:
                window = [(0, k[0], 3)]
            return window + [(3, LT, 1), (4, LT + 1, 1)]

        def scores(self, t0=0, n=None):
            n = n_keys[self.kind] if n is None else n
            return pl.ps[:, 1536 * self.par + t0 * P:1536 * self.par + (t0 + n) * P]

        def own(self, g):
            return g == 1

        def turned_bank(self, g):
            return 3 * self.par if self.own(g) else 6

        def before_in_bank_6(self, g):
            w = self
            while True:
                g -= 1
                if g < 0:
                    w = w.step(-1)
                    if w is None:
                        return None
                    g = len(groups[w.kind]) - 1
                if not w.own(g):
                    return w, g

    def over_units(eng, body):
        for lo, hi in segments:
            if hi - lo > 1:
                with eng.Fori(lo, hi) as b:
                    for h in range(HEADS):
                        body(Unit(lo, b, h))
            else:
                for h in range(HEADS):
                    body(Unit(lo, lo, h))

    final = Unit(len(blocks) - 1, len(blocks) - 1, HEADS - 1)

    with nc.Block() as block:
        @block.gpsimd
        def _(pool):
            for p0 in (0, HD):
                h0 = 2 - 2 * (p0 // HD)
                for z in (q_hi, q_lo):
                    pool.memset(raw(z[p0:p0 + HD, h0:h0 + 2, :]), 0.0).then_inc(q_ready, 1)
            for lo, hi in segments:
                def stage(b):
                    g = blocks[lo][2]
                    i = b - g * tiles
                    src = pl.qk[:, 3 * g:3 * g + 2, :].rearrange("p k (t q) -> p k t q", q=P)
                    for p0 in (0, HD):
                        h0 = 2 * (p0 // HD)
                        part = lambda z: z[p0:p0 + HD, h0:h0 + 2, :]
                        n = b * 2 + h0 // 2
                        if not (isinstance(b, int) and b == 0 and p0 == 0):
                            pool.wait_ge(q_ready, n + 4)
                        pool.tensor_copy(part(qst), src[p0:p0 + HD, :, i, :]).then_inc(q_staged, 1)
                        if not (isinstance(b, int) and b == 0):
                            pool.wait_ge(s_full, b * HEADS + (h0 - 2))
                        pool.wait_ge(q_staged, n + 1)
                        one = pl.small[p0:p0 + HD, 2:3].unsqueeze(2).broadcast_to([HD, 2, P])
                        pool.tensor_tensor(part(q_hi), part(qst), one, ALU.mult).then_inc(q_rounded, 1)
                        pool.wait_ge(q_rounded, n + 1)
                        pool.tensor_tensor(part(q_lo), part(qst), raw(part(q_hi)), ALU.subtract) \
                            .then_inc(q_ready, 1)
                if hi - lo > 1:
                    with pool.Fori(lo, hi) as b:
                        stage(b)
                else:
                    stage(lo)

        @block.tensor
        def _(pe):
            def wait_copied(w, g):
                if g == 0:
                    pe.wait_ge(first_copied, w.u + 1)
                else:
                    pe.wait_ge(later_copied, w.late + g)

            def score(w):
                if w.h % 2 == 0:
                    pe.wait_ge(q_ready, w.b * 2 + (5 + w.h // 2))
                if w.static and w.h == 0 and w.r in (0, tiles):
                    pe.wait_ge(k_split, 2 if w.r else 1)
                if not (w.static and w.u < 2):
                    v = w.step(-2)
                    for g in range(len(groups[v.kind])):
                        if v.own(g):
                            wait_copied(v, g)
                if not (w.static and w.u < 2):
                    pe.wait_ge(p_done, w.u - 1)
                parts = [z.rearrange("p (t k) -> p t k", k=P)
                         for z in (k_hi[:, w.group, :], k_lo[:, 3 * w.group + 2, :])]
                for place, tile, n in w.runs():
                    out = w.scores(place, n).rearrange("p (t k) -> p t k", k=P)
                    hi, lo = (z[:, bass.ds(tile, n), :] for z in parts)
                    mm = three_pass(pe, out, q_hi[:, w.h, :], q_lo[:, w.h, :], hi, lo, True, True)
                mm.then_inc(s_full, 1)

            def transposes(w, g):
                first, end = groups[w.kind][g]
                if g == 0:
                    pe.wait_ge(p_done, w.u + 1)
                before = None if w.own(g) else w.before_in_bank_6(g)
                if before is not None:
                    wait_copied(*before)
                for t in range(first, end):
                    tr = pe.transpose(pl.bank(w.turned_bank(g))[:, (t - first) * P:(t - first + 1) * P],
                                      prob[w.par][:, t * P:(t + 1) * P], pl.c(IDENT))
                tr.then_inc(t_full, 1)

            def values(w, g):
                first, end = groups[w.kind][g]
                if g == 0:
                    pe.wait_ge(first_copied, w.u + 1)
                    if not (w.static and w.u < 1):
                        pe.wait_ge(o_done, w.u)
                else:
                    pe.wait_ge(later_copied, w.late + g)
                keys = w.keys()
                col = 128 * w.group + HD * (w.h // 2)
                for t in range(first, end):
                    mm = pe.matmul(pl.bank(7, HD), turned[w.par][:, t * P:(t + 1) * P],
                                   pl.v[:, keys[t], col:col + HD], start=(t == 0),
                                   stop=(t == len(keys) - 1))
                if end == len(keys):
                    mm.then_inc(pv_done, 1)

            score(Unit(0, 0, 0))
            score(Unit(0, 0, 1))

            def body(w):
                second, prev = w.step(2), w.step(-1)
                for g in range(len(groups[w.kind])):
                    if w.kind != "A":
                        transposes(w, g)
                    elif g == 0:
                        transposes(w, 0)
                        transposes(w, 1)
                    if prev is not None and g < len(groups[prev.kind]):
                        values(prev, g)
                if prev is not None:
                    for g in range(len(groups[w.kind]), len(groups[prev.kind])):
                        values(prev, g)
                if second is not None:
                    score(second)
            over_units(pe, body)
            for g in range(len(groups[final.kind])):
                values(final, g)

        @block.vector
        def _(dve):
            def maximum(w):
                dve.wait_ge(s_full, w.u + 1)
                if w.kind == "A":
                    if w.static:
                        variant = 0 if w.i == 0 else 2 if w.i == LT - 1 else 1
                    else:
                        variant = 1
                    win = w.scores(0, 3)
                    dve.tensor_tensor(win, win, pl.c(MASKS + 3 * P * variant, 3 * P), ALU.add) \
                        .then_inc(masked, 1)
                    dve.wait_ge(masked, w.u + 1)
                dve.tensor_reduce(mx[w.h], w.scores(), AX.X, ALU.max).then_inc(maxed, 1)
                dve.wait_ge(maxed, w.u + 1)
                if w.group == 0:
                    dve.tensor_scalar(nm[w.h], mx[w.h], -SCALE, nsink[:, w.h:w.h + 1],
                                      ALU.mult, ALU.min).then_inc(nm_done, 1)
                else:
                    dve.tensor_scalar(nm[w.h], mx[w.h], -SCALE, None, ALU.mult).then_inc(nm_done, 1)

            def copy_first(w):
                end = groups[w.kind][0][1]
                dve.wait_ge(t_full, w.all + 1)
                dve.tensor_copy(turned[w.par][:, 0:end * P], pl.bank(w.turned_bank(0), end * P)) \
                    .then_inc(first_copied, 1)

            def output(w):
                if w.group == 0:
                    dve.wait_ge(es_done, w.u + 1)
                    dve.tensor_tensor(dn[w.h], den[w.h], es[w.h], ALU.add).then_inc(dn_done, 1)
                    dve.wait_ge(dn_done, w.u + 1)
                    dve.reciprocal(rd[w.h], dn[w.h]).then_inc(rd_done, 1)
                else:
                    dve.reciprocal(rd[w.h], den[w.h]).then_inc(rd_done, 1)
                dve.wait_ge(rd_done, w.u + 1)
                dve.wait_ge(pv_done, w.u + 1)
                col = HEADS * HD * w.group + HD * w.h
                dve.tensor_scalar(pl.mixab[:, w.i, col:col + HD], pl.bank(7, HD), rd[w.h], None,
                                  ALU.mult).then_inc(o_done, 1)

            for g in range(2):
                k = pl.qk[:, 3 * g + 2, :]
                dve.wait_ge(k_rounded, g + 1)
                dve.tensor_tensor(k_lo[:, 3 * g + 2, :], k, raw(k_hi[:, g, :]), ALU.subtract) \
                    .then_inc(k_split, 1)
            dve.tensor_scalar(nsink, pl.prm[:, SINK:SINK + HEADS], -1.0, None, ALU.mult) \
                .then_inc(nsink_done, 1)
            dve.wait_ge(nsink_done, 1)
            maximum(Unit(0, 0, 0))

            def body(w):
                nxt, prev = w.step(1), w.step(-1)
                if nxt is not None:
                    maximum(nxt)
                if w.kind != "A":
                    copy_first(w)
                if prev is not None:
                    output(prev)
            over_units(dve, body)
            output(final)

        @block.scalar
        def _(act):
            def exponent(w):
                act.wait_ge(nm_done, w.u + 1)
                if not (w.static and w.u < 2):
                    act.wait_ge(t_full, w.step(-1).all)
                if not (w.static and w.u < HEADS):
                    act.wait_ge(o_done, w.u - (HEADS - 1))
                act.activation(prob[w.par][:, 0:n_keys[w.kind] * P], w.scores(), ACT.Exp, bias=nm[w.h],
                               scale=SCALE, accum_out=den[w.h]).then_inc(p_done, 1)
                if w.group == 0:
                    act.activation(es[w.h], pl.prm[:, SINK + w.h:SINK + w.h + 1], ACT.Exp,
                                   bias=nm[w.h]).then_inc(es_done, 1)

            for g in range(2):
                act.activation(k_hi[:, g, :], pl.qk[:, 3 * g + 2, :], ACT.Copy).then_inc(k_rounded, 1)
            exponent(Unit(0, 0, 0))

            def body(w):
                nxt = w.step(1)
                for g in range(0 if w.kind == "A" else 1, len(groups[w.kind])):
                    first, end = groups[w.kind][g]
                    act.wait_ge(t_full, w.all + (g + 1))
                    act.activation(turned[w.par][:, first * P:end * P],
                                   pl.bank(w.turned_bank(g), (end - first) * P), ACT.Copy) \
                        .then_inc(later_copied if g else first_copied, 1)
                if nxt is not None:
                    exponent(nxt)
            over_units(act, body)



def project_ssd(pl, l, last):
    nc, a = pl.nc, pl.a
    tag = f"c{l}"
    kinds = ["z"] * 4 + ["x"] * 4 + ["b"] * 2 + ["s"] * 2 + ["dt"]
    chunks_of = lambda kind: (0, 1) if last and kind == "z" else ORDER
    order_of = lambda kind: [c for c in ORDER if c in chunks_of(kind)]
    segments = [(1, kinds[2 * n:2 * n + 2]) for n in range(7)]
    ring = Ring(pl, tag)
    full = [pl.sem(f"{tag}_full{c}") for c in range(3)]
    taken = [pl.sem(f"{tag}_taken{c}") for c in range(3)]
    pad = [pl.at(f"{tag}_pad{s}", [P, TOK + 8], F32, kb=150 + 5.25 * s) for s in range(2)]
    u = pl.at(f"{tag}_u", [P, TOK], F32, kb=161)
    zs = pl.at(f"{tag}_zs", [P, TT, P], F32, kb=161)
    cleared = pl.sem(f"{tag}_cleared")
    tapped = pl.sem(f"{tag}_tapped")
    smooth = pl.sem(f"{tag}_smooth")
    turned = pl.sem(f"{tag}_turned")
    stored = pl.sem(f"{tag}_stored")
    z_out = pl.sem(f"{tag}_z_out")

    turns = {n: [] for n in range(13)}
    for n, kind in enumerate(kinds):
        of = n if kind in ("z", "dt") else n - 1
        if of >= 0 and (of == n or kinds[of] in ("x", "b")):
            turns[n] = [(of, c) for c in order_of(kinds[of])]
    flat = [x for n in range(13) for x in turns[n]]
    number = {x: q for q, x in enumerate(flat)}
    through = {of: max(q for x, q in number.items() if x[0] == of) + 1 for of, _ in flat}
    parts = ((SEQ, CTX, (2,)), (0, 510, (0,)), (510, 514, (0, 1)))
    per_block = len(parts) * CONV

    def count(of, c):
        return sum(c in chunks_of(k) for k in kinds[:of + 1])

    with nc.Block() as block:
        @block.sync
        def _(sp):
            def z_store(n):
                sp.wait_ge(stored, through[n] + 2)
                width = SEQ // P if last else TT
                sp.dma_start(pl.z_dram[:, 0:width, n * P:(n + 1) * P], zs[:, 0:width, :]) \
                    .then_inc(z_out, 16)

            def body(at):
                ring.load(sp, at, a["w_in"][l, 8 + at.n])
                if 2 <= at.n < 6:
                    z_store(at.n - 2)
            over(sp, segments, chunks_of, body)
            sp.wait_ge(z_out, 64)

        @block.gpsimd
        def _(pool):
            pool.sem_inc(ring.ready, 2)
            for s in range(2):
                pool.memset(pad[s][:, 0:2], 0.0)
                pool.memset(pad[s][:, SEQ + 2:SEQ + 6], 0.0)
                pool.memset(pad[s][:, TOK + 6:TOK + 8], 0.0).then_inc(cleared, 1)
            pool.wait_ge(ring.ready, 4)
            over(pool, segments[1:], chunks_of, lambda at: ring.split(pool, at, full[1]), start=2)

        @block.tensor
        def _(pe):
            pe.sem_inc(full[1], 2)

            def body(at):
                multiply_block(pl, pe, ring, at, chunks_of(at.kind), full, taken)
                for of, c in turns[at.n]:
                    q = number[of, c]
                    if kinds[of] in ("z", "dt"):
                        src = pad[of % 2]
                        pe.wait_ge(taken[c], count(of, c) + 2)
                    else:
                        pe.wait_ge(smooth, of - 3)
                    pe.wait_ge(stored, q + 1)
                    for t in range(CHUNKS[c][1] // P):
                        tok = CHUNKS[c][0] + t * P
                        if kinds[of] in ("z", "dt"):
                            src = pad[of % 2][:, PADDED[c] + t * P:PADDED[c] + (t + 1) * P]
                        elif kinds[of] == "x":
                            src = u[:, tok:tok + P]
                        else:
                            src = pl.bt[:, of - 8, tok:tok + P]
                        tr = pe.transpose(pl.bank(6 + q % 2)[:, t * P:(t + 1) * P], src, pl.c(IDENT))
                    tr.then_inc(turned, 1)
            over(pe, segments, chunks_of, body)


        @block.scalar
        def _(act):
            for c in range(3):
                act.sem_inc(taken[c], 2)
            act.sem_inc(stored, 2)
            ring.round_first(act)

            def take(at, c):
                if c not in chunks_of(at.kind):
                    return
                tn = CHUNKS[c][1]
                wait_full(act, full, at, c)
                if at.n >= 6 and at.n < 12:
                    act.wait_ge(tapped, (at.n - 5) * per_block)
                elif at.n == 12:
                    act.wait_ge(tapped, 7 * per_block)
                act.activation(pad[at.par][:, PADDED[c]:PADDED[c] + tn], pl.bank(3 * at.par + c, tn),
                               ACT.Silu if at.kind == "z" else ACT.Copy).then_inc(taken[c], 1)

            def store(of, c):
                q = number[of, c]
                t0, tn = CHUNKS[c]
                tt = slice(t0 // P, (t0 + tn) // P)
                act.wait_ge(turned, q + 1)
                src = pl.bank(6 + q % 2, tn).rearrange("p (t d) -> p t d", d=P)
                if kinds[of] == "z":
                    if of >= 1:
                        act.wait_ge(z_out, 16 * of)
                    dst = zs[:, tt, :]
                elif kinds[of] == "dt":
                    dst, src = pl.dtr[:, tt, :], src[:, :, P - 2 * CH:P]
                else:
                    dst = pl.xb[:, tt, (of - 4) * P:(of - 3) * P]
                act.activation(dst, src, ACT.Copy).then_inc(stored, 1)

            def body(at):
                take(at, 2)
                take(at, 0)
                if at.n >= 5:
                    m = at.n - 5
                    act.wait_ge(tapped, (m + 1) * per_block)
                    kind = kinds[at.n - 1]
                    dst = u[:, :] if kind == "x" else pl.bt[:, m - 4, :] if kind == "b" else pl.ct[:, m - 6, :]
                    act.activation(dst, u[:, :], ACT.Silu).then_inc(smooth, 1)
                take(at, 1)
                for of, c in turns[at.n]:
                    store(of, c)
            over(act, segments, chunks_of, body)

        @block.vector
        def _(dve):
            ring.rest_first(dve)
            dve.wait_ge(cleared, 2)
            dve.wait_ge(z_out, 64)
            for m in range(8):
                n = m + 4
                w = pl.prm[:, CONVW + CONV * m:CONVW + CONV * (m + 1)]
                if m >= 1:
                    if kinds[n - 1] == "x":
                        dve.wait_ge(turned, through[n - 1])
                    else:
                        dve.wait_ge(smooth, m)
                for j in range(CONV):
                    for q, (t0, tn, need) in enumerate(parts):
                        if j == 0:
                            for c in need:
                                dve.wait_ge(taken[c], count(n, c) + 2)
                        s0 = t0 + j + (4 if t0 == SEQ else 0)
                        src, out = pad[n % 2][:, s0:s0 + tn], u[:, t0:t0 + tn]
                        if j == 0:
                            dve.tensor_scalar(out, src, w[:, 0:1], pl.prm[:, CONVB + m:CONVB + m + 1],
                                              ALU.mult, ALU.add).then_inc(tapped, 1)
                        else:
                            dve.wait_ge(tapped, m * per_block + (j - 1) * len(parts) + q + 1)
                            dve.scalar_tensor_tensor(out=out, in0=src, scalar=w[:, j:j + 1], in1=out,
                                                     op0=ALU.mult, op1=ALU.add).then_inc(tapped, 1)



def scan(pl, l, last):
    nc = pl.nc
    tag = f"s{l}"
    at = pl.at
    hb = at(f"{tag}_hb", [P, TT + 1, 512], F32, kb=0)
    zt = [at(f"{tag}_z{s}", [P, 512], F32, kb=22 + 2 * s) for s in range(2)]
    up_f, up_b = (at(f"{tag}_up{d}", [P, CH, P], F32, kb=26 + 4 * d) for d in range(2))
    both = lambda name, shape, kb0, kb1: [at(f"{tag}_{name}{s}", [P, *shape], F32, kb=kb)
                                          for s, kb in enumerate((kb0, kb1))]
    e_f, e_b = both("ef", [CH, P], 34, 170), both("eb", [CH, P], 38, 174)
    xd_f, xd_b, xfe = both("xdf", [512], 42, 178), both("xdb", [512], 44, 180), both("xfe", [512], 46, 182)
    hf = [at(f"{tag}_hf{s}", [P, 512], F32, kb=48 + 2 * s) for s in range(2)]
    b_st, c_st = both("bst", [GROUPS, P], 52, 184), both("cst", [GROUPS, P], 53, 185)
    b_tok = both("btok", [GROUPS, P], 54, 186)
    g_f, g_b = (at(f"{tag}_g{d}", [P, GROUPS, P], F32, kb=55 + d) for d in range(2))
    t1, t2 = (at(f"{tag}_t{d}", [P, 512], F32, kb=57 + 2 * d) for d in range(2))
    xskip = both("skip", [512], 61, 187)
    dt, dta, dend, eac, cdec, wde, tmp, tmp2, tmp3 = (
        at(f"{tag}_d{d}", [P, TT, 2 * CH], F32, kb=63 + 0.625 * d) for d in range(9))
    av = at(f"{tag}_av", [P, 2 * CH], F32, kb=69)
    xde = [at(f"{tag}_xde{s}", [P, 512], F32, kb=70 + 2 * s) for s in range(2)]
    b_tok1 = [at(f"{tag}_bt{s}", [P, 256], F32, kb=74 + s) for s in range(2)]
    sq = at(f"{tag}_sq", [P, 512], F32, kb=76)
    FW, BW = slice(0, CH), slice(CH, 2 * CH)

    def sem(name):
        return pl.sem(f"{tag}_{name}")
    step, summed, acted = sem("step"), sem("summed"), sem("acted")

    def heads(t):
        return t.rearrange("p (h d) -> p h d", h=CH)

    def per_head(t, c, cols):
        return t[:, c, cols].unsqueeze(2).broadcast_to([P, CH, HD])

    with nc.Block() as block:
        @block.vector
        def _(dve):
            done = [0]

            def chain(ins):
                done[0] += 1
                ins.then_inc(step, 1)
                dve.wait_ge(step, done[0])
            bias = pl.prm[:, DTB:DTB + 2 * CH].unsqueeze(1).broadcast_to([P, TT, 2 * CH])
            chain(dve.tensor_tensor(tmp[:, :, :], pl.dtr[:, :, :], bias, ALU.add))
            chain(dve.scalar_tensor_tensor(out=tmp2[:, :, :], in0=tmp[:, :, :], scalar=-1.0,
                                           in1=tmp[:, :, :], op0=ALU.mult, op1=ALU.max))
            dve.wait_ge(acted, 1)
            chain(dve.tensor_scalar(tmp2[:, :, :], tmp3[:, :, :], 1.0, None, ALU.add))
            chain(dve.tensor_scalar(dend[:, :, :], tmp2[:, :, :], -1.0, None, ALU.add))
            chain(dve.tensor_tensor(dend[:, :, :], tmp3[:, :, :], dend[:, :, :], ALU.subtract))
            chain(dve.reciprocal(eac[:, :, :], tmp2[:, :, :]))
            chain(dve.tensor_tensor(dend[:, :, :], dend[:, :, :], eac[:, :, :], ALU.mult))
            dve.wait_ge(acted, 2)
            chain(dve.tensor_tensor(dend[:, :, :], dend[:, :, :], cdec[:, :, :], ALU.add))
            chain(dve.scalar_tensor_tensor(out=dt[:, :, :], in0=tmp[:, :, :], scalar=0.0,
                                           in1=dend[:, :, :], op0=ALU.max, op1=ALU.add))
            dve.wait_ge(acted, 3)
            chain(dve.scalar_tensor_tensor(out=dta[:, :, :], in0=dt[:, :, :], scalar=-1.0,
                                           in1=av[:, :].unsqueeze(1).broadcast_to([P, TT, 2 * CH]),
                                           op0=ALU.mult, op1=ALU.mult))
            dve.wait_ge(acted, 8)
            dve.tensor_tensor(wde[:, :, :], dt[:, :, :], dend[:, :, :], ALU.mult)
            dve.memset(hb[:, 0, :], 0.0)
            dve.memset(hf[0][:, :], 0.0)

        @block.scalar
        def _(act):
            act.wait_ge(step, 2)
            act.activation(tmp3[:, :, :], tmp2[:, :, :], ACT.Exp, scale=-1.0).then_inc(acted, 1)
            act.wait_ge(step, 3)
            act.activation(cdec[:, :, :], tmp2[:, :, :], ACT.Ln).then_inc(acted, 1)
            act.activation(av[:, :], pl.prm[:, ALOG:ALOG + 2 * CH], ACT.Exp).then_inc(acted, 1)
            act.wait_ge(summed, 5)
            for j, (dst, cols) in enumerate(((dend, FW), (dend, BW), (eac, FW), (eac, BW),
                                             (cdec, slice(0, 2 * CH)))):
                src = pl.bank(j, TT * 2 * CH).rearrange("p (t h) -> p t h", t=TT)
                act.activation(dst[:, :, cols], src[:, :, cols], ACT.Exp).then_inc(acted, 1)

        @block.tensor
        def _(pe):
            pe.wait_ge(step, 10)
            rhs = dta[:, :, :].rearrange("p t h -> p (t h)")
            for j, m in enumerate((AFTER, BEFORE, UPTO, FROM, ONES)):
                pe.matmul(pl.bank(j, TT * 2 * CH), pl.c(m), rhs, start=True, stop=True).then_inc(summed, 1)

    copied1 = sem("copied1")
    staged1, s_full, scaled1, h_done = sem("staged1"), sem("s_full"), sem("scaled1"), sem("h_done")
    xb = pl.xb
    pairs = ((0, 1), (1, TT // 2))

    def over_pairs(eng, body):
        for lo, hi in pairs:
            if hi - lo > 1:
                with eng.Fori(lo, hi) as i:
                    for s in range(2):
                        body(i * 2 + s, s, False, i)
            else:
                for s in range(2):
                    body(s, s, True, 0)

    with nc.Block() as block:
        @block.gpsimd
        def _(pool):
            def body(o, s, first, i):
                c = (i * -2) + (TT - 1 - s)
                if not first:
                    pool.wait_ge(s_full, o - 1)
                pool.tensor_tensor(heads(xde[s][:, :]), heads(xb[:, c, 0:512]), per_head(wde, c, BW),
                                   ALU.mult).then_inc(staged1, 1)
            over_pairs(pool, body)

        @block.scalar
        def _(act):
            def body(o, s, first, i):
                c = (i * -2) + (TT - 1 - s)
                if not first:
                    act.wait_ge(s_full, o - 1)
                act.activation(b_tok1[s][:, :], xb[:, c, 512:768], ACT.Copy).then_inc(copied1, 1)
            over_pairs(act, body)

        @block.tensor
        def _(pe):
            def body(o, s, first, i):
                pe.wait_ge(staged1, o + 1)
                pe.wait_ge(copied1, o + 1)
                if not first:
                    pe.wait_ge(h_done, o - 1)
                for g in range(GROUPS):
                    mm = pe.matmul(pl.bank(s)[:, 256 * g:256 * (g + 1)], b_tok1[s][:, P * g:P * (g + 1)],
                                   xde[s][:, 256 * g:256 * (g + 1)], start=True, stop=True)
                mm.then_inc(s_full, 1)
            over_pairs(pe, body)

        @block.vector
        def _(dve):
            def body(o, s, first, i):
                c = (i * -2) + (TT - 1 - s)
                if not (first and s == 0):
                    dve.wait_ge(h_done, o)
                dve.tensor_tensor(heads(hb[:, o + 1, :]), heads(hb[:, o, :]), per_head(cdec, c, BW),
                                  ALU.mult).then_inc(scaled1, 1)
                dve.wait_ge(scaled1, o + 1)
                dve.wait_ge(s_full, o + 1)
                dve.tensor_tensor(hb[:, o + 1, :], hb[:, o + 1, :], pl.bank(s), ALU.add) \
                    .then_inc(h_done, 1)
            over_pairs(dve, body)

    z_in = [sem(f"z_in{s}") for s in range(2)]
    names = ("staged", "btok_in", "xfe_in", "xd_in", "skip_in", "up_in", "seg_full", "exp_done",
             "g_full", "g_done", "e_done", "st_full", "h_scaled", "hf_done", "off_full", "diag_full",
             "y1", "y2", "y3", "y4", "y5", "y_done", "sq_done")
    q = {n: sem(n) for n in names}

    with nc.Block() as block:
        def step_at(o, s, i):
            if isinstance(i, int) and i == 0:
                return (s, s, LT + s, None if last else s, 0)
            return (o, s, i * 2 + (s - 2), i * 2 + (s - (2 if last else 0)), i)

        def over_chunks(eng, body):
            n = (LT + 2) // 2
            for lo, hi in ((0, 1), (1, n - 1), (n - 1, n)):
                def pair(i):
                    for s in range(2):
                        v = step_at(i * 2 + s, s, i)
                        w = step_at(i * 2 + 1, 1, i) if s == 0 else step_at(i * 2 + 2, 0, i + 1)
                        body(v, None if lo == n - 1 and s == 1 else w)
                if hi - lo > 1:
                    with eng.Fori(lo, hi) as i:
                        pair(i)
                else:
                    pair(lo)

        def before(number, back):
            return not isinstance(number, int) or number >= back

        @block.sync
        def _(sp):
            def body(v, w):
                o, s, c, y, i = v
                if y is not None:
                    sp.wait_ge(q["y_done"], y + 1)
                    sp.dma_start(zt[s][:, :], pl.z_dram[:, c, :]).then_inc(z_in[s], 16)
            over_chunks(sp, body)

        @block.gpsimd
        def _(pool):
            def body(v, w):
                o, s, c, y, i = v
                x = heads(xb[:, c, 0:512])
                if before(o, 2):
                    pool.wait_ge(q["st_full"], o - 1)
                pool.tensor_copy(b_tok[s][:, :, :].rearrange("p g n -> p (g n)"), xb[:, c, 512:768]) \
                    .then_inc(q["btok_in"], 1)
                pool.tensor_tensor(heads(xfe[s][:, :]), x, per_head(wde, c, FW), ALU.mult) \
                    .then_inc(q["xfe_in"], 1)
                if y is None:
                    return
                pool.wait_ge(q["y_done"], y + 1)
                cs = lambda t: t[:, :, :].rearrange("p g (t n) -> p g t n", n=P)[:, :, c, :]
                pool.tensor_copy(b_st[s][:, :, :], cs(pl.bt)).then_inc(q["staged"], 1)
                pool.tensor_copy(c_st[s][:, :, :], cs(pl.ct)).then_inc(q["staged"], 1)
                pool.tensor_tensor(heads(xd_f[s][:, :]), x, per_head(dt, c, FW), ALU.mult) \
                    .then_inc(q["xd_in"], 1)
                pool.tensor_tensor(heads(xd_b[s][:, :]), x, per_head(dt, c, BW), ALU.mult) \
                    .then_inc(q["xd_in"], 1)
                skip_w = pl.prm[:, DSKIP:DSKIP + CH].unsqueeze(2).broadcast_to([P, CH, HD])
                pool.tensor_tensor(heads(xskip[s][:, :]), x, skip_w, ALU.mult).then_inc(q["skip_in"], 1)
            over_chunks(pool, body)

        @block.tensor
        def _(pe):
            def seg(w):
                y = w[3]
                for d, (m, up) in enumerate(((AFTER, up_f), (BEFORE, up_b))):
                    if before(y, 1):
                        pe.wait_ge(q["exp_done"], y * 2 + (d - 1))
                    pe.wait_ge(q["up_in"], y * 2 + (d + 1))
                    for g in range(GROUPS):
                        mm = pe.matmul(pl.bank(2 * d + g), pl.c(m),
                                       up[:, 4 * g:4 * g + 4, :].rearrange("p h l -> p (h l)"),
                                       start=True, stop=True)
                    mm.then_inc(q["seg_full"], 1)

            if not last:
                seg(step_at(0, 0, 0))

            def body(v, w):
                o, s, c, y, i = v
                if before(o, 1):
                    pe.wait_ge(q["hf_done"], o)
                if y is not None:
                    pe.wait_ge(q["staged"], y * 2 + 2)
                    for g in range(GROUPS):
                        mm = pe.matmul(pl.bank(4)[:, P * g:P * (g + 1)], b_st[s][:, g, :],
                                       c_st[s][:, g, :], start=True, stop=True)
                    mm.then_inc(q["g_full"], 1)
                    if before(y, 1):
                        pe.wait_ge(q["y2"], y)
                    for d, (bank, h) in enumerate(((6, hf[s][:, :]), (7, hb[:, (c * -1) + (TT - 1), :]))):
                        for g in range(GROUPS):
                            mm = pe.matmul(pl.bank(bank)[:, 256 * g:256 * (g + 1)], c_st[s][:, g, :],
                                           h[:, 256 * g:256 * (g + 1)], start=True, stop=True)
                        mm.then_inc(q["off_full"], 1)
                    pe.wait_ge(q["g_done"], y * 2 + 2)
                pe.wait_ge(q["btok_in"], o + 1)
                pe.wait_ge(q["xfe_in"], o + 1)
                for g in range(GROUPS):
                    mm = pe.matmul(pl.bank(4)[:, 256 * g:256 * (g + 1)], b_tok[s][:, g, :],
                                   xfe[s][:, 256 * g:256 * (g + 1)], start=True, stop=True)
                mm.then_inc(q["st_full"], 1)
                if y is not None:
                    pe.wait_ge(q["e_done"], y * 2 + 2)
                    pe.wait_ge(q["xd_in"], y * 2 + 2)
                    if before(y, 1):
                        pe.wait_ge(q["y5"], y)
                    for h in range(CH):
                        out = pl.bank(5)[:, HD * h:HD * (h + 1)]
                        pe.matmul(out, e_f[s][:, h, :], xd_f[s][:, HD * h:HD * (h + 1)], start=True,
                                  stop=False)
                        mm = pe.matmul(out, e_b[s][:, h, :], xd_b[s][:, HD * h:HD * (h + 1)],
                                       start=False, stop=True)
                    mm.then_inc(q["diag_full"], 1)
                if w is not None and w[3] is not None:
                    seg(w)
            over_chunks(pe, body)

        @block.scalar
        def _(act):
            def exponents(w):
                y = w[3]
                if before(y, 2):
                    act.wait_ge(q["diag_full"], y - 1)
                for d, e in enumerate((e_f[w[1]], e_b[w[1]])):
                    act.wait_ge(q["seg_full"], y * 2 + (d + 1))
                    act.activation(e[:, :, :].rearrange("p h l -> p (h l)"),
                                   pl.ps[:, 1024 * d:1024 * (d + 1)], ACT.Exp).then_inc(q["exp_done"], 1)

            if not last:
                exponents(step_at(0, 0, 0))

            def body(v, w):
                o, s, c, y, i = v
                if w is not None and w[3] is not None:
                    exponents(w)
                if y is None:
                    return
                if before(y, 1):
                    act.wait_ge(q["sq_done"], y * 2)
                act.wait_ge(q["y_done"], y + 3)
                for g in range(GROUPS):
                    act.activation(sq[:, 256 * g:256 * (g + 1)], pl.mixc[:, c, 256 * g:256 * (g + 1)],
                                   ACT.Square, accum_out=pl.ssq[:, c, g:g + 1]).then_inc(q["sq_done"], 1)
            over_chunks(act, body)

        @block.vector
        def _(dve):
            def ups(w):
                c, y = w[2], w[3]
                for d, (m, up, cols) in enumerate(((UPTO, up_f, FW), (FROM, up_b, BW))):
                    if before(y, 1):
                        dve.wait_ge(q["seg_full"], y * 2 + (d - 1))
                    dve.tensor_tensor(up[:, :, :], pl.c(m).unsqueeze(1).broadcast_to([P, CH, P]),
                                      dta[:, c, cols].unsqueeze(2).broadcast_to([P, CH, P]),
                                      ALU.mult).then_inc(q["up_in"], 1)

            dve.sem_inc(q["y_done"], 2)
            if not last:
                ups(step_at(0, 0, 0))

            def body(v, w):
                o, s, c, y, i = v
                if y is not None:
                    dve.wait_ge(q["g_full"], y + 1)
                    if before(y, 1):
                        dve.wait_ge(q["e_done"], y * 2)
                    gp = pl.bank(4, 256).rearrange("p (g l) -> p g l", g=GROUPS)
                    for m, g in ((UPTO, g_f), (FROM, g_b)):
                        dve.tensor_tensor(g[:, :, :], gp, pl.c(m).unsqueeze(1).broadcast_to([P, GROUPS, P]),
                                          ALU.mult).then_inc(q["g_done"], 1)
                if y is not None:
                    dve.wait_ge(q["g_done"], y * 2 + 2)
                    for d, (e, g) in enumerate(((e_f[s], g_f), (e_b[s], g_b))):
                        dve.wait_ge(q["exp_done"], y * 2 + (d + 1))
                        for k in range(GROUPS):
                            ins = dve.tensor_tensor(e[:, 4 * k:4 * k + 4, :], e[:, 4 * k:4 * k + 4, :],
                                                    g[:, k, :].unsqueeze(1).broadcast_to([P, 4, P]), ALU.mult)
                        ins.then_inc(q["e_done"], 1)
                dve.tensor_tensor(heads(hf[1 - s][:, :]), heads(hf[s][:, :]), per_head(cdec, c, FW),
                                  ALU.mult).then_inc(q["h_scaled"], 1)
                dve.wait_ge(q["h_scaled"], o + 1)
                dve.wait_ge(q["st_full"], o + 1)
                dve.tensor_tensor(hf[1 - s][:, :], hf[1 - s][:, :], pl.bank(4), ALU.add) \
                    .then_inc(q["hf_done"], 1)
                if w is not None and w[3] is not None:
                    ups(w)
                dve.wait_ge(q["hf_done"], o + 1)
                if y is None:
                    return
                dve.wait_ge(q["off_full"], y * 2 + 2)
                dve.tensor_tensor(heads(t1[:, :]), heads(pl.bank(6)), per_head(eac, c, FW), ALU.mult) \
                    .then_inc(q["y1"], 1)
                dve.tensor_tensor(heads(t2[:, :]), heads(pl.bank(7)), per_head(eac, c, BW), ALU.mult) \
                    .then_inc(q["y2"], 1)
                dve.wait_ge(q["y1"], y + 1)
                dve.wait_ge(q["y2"], y + 1)
                dve.tensor_tensor(t1[:, :], t1[:, :], t2[:, :], ALU.add).then_inc(q["y3"], 1)
                dve.wait_ge(q["y3"], y + 1)
                dve.wait_ge(q["skip_in"], y + 1)
                dve.tensor_tensor(t1[:, :], t1[:, :], xskip[s][:, :], ALU.add).then_inc(q["y4"], 1)
                dve.wait_ge(q["y4"], y + 1)
                dve.wait_ge(q["diag_full"], y + 1)
                dve.tensor_tensor(t1[:, :], t1[:, :], pl.bank(5), ALU.add).then_inc(q["y5"], 1)
                dve.wait_ge(q["y5"], y + 1)
                dve.wait_ge(z_in[s], (i - (1 if last else 0)) * 16 + 16)
                dve.tensor_tensor(pl.mixc[:, c, :], t1[:, :], zt[s][:, :], ALU.mult).then_inc(q["y_done"], 1)
            over_chunks(dve, body)



def gather_mix(pl, l, last):
    tag = f"gm{l}"
    tiles = LT if last else TT
    chunks = (0, 1) if last else (0, 1, 2)
    width = SEQ if last else TOK
    rs = pl.at(f"{tag}_rs", [P, 2, TT, GROUPS], F32, kb=194)
    rooted, inverted, normed, x_in, turned, rounded, rest = (
        pl.sem(f"{tag}_{x}") for x in ("rooted", "inverted", "normed", "x_in", "turned", "rounded", "rest"))
    items = [(k, c) for k in range(KT) for c in chunks]

    def gain(k):
        return pl.prm[:, GNORM + k - 4:GNORM + k - 3]

    def sync(sp):
        sp.dma_start(pl.x[:, :, 0:width], pl.x_dram[:, :, 0:width]).then_inc(x_in, 16)

    def scalar(act):
        act.activation(rs[:, 0, 0:tiles, :], pl.ssq[:, 0:tiles, :], ACT.Sqrt, scale=1.0 / 256.0,
                       bias=pl.small[:, 0:1]).then_inc(rooted, 1)
        for n, (k, c) in enumerate(items):
            t0, tn = CHUNKS[c]
            act.wait_ge(turned, n + 1)
            act.activation(pl.hi[:, k, t0:t0 + tn], pl.bank(n % 8, tn), ACT.Copy,
                           scale=1.0 if k < 4 else gain(k)).then_inc(rounded, 1)

    def tensor(pe):
        for n, (k, c) in enumerate(items):
            t0, tn = CHUNKS[c]
            if k == 4 and c == 0:
                pe.wait_ge(normed, tiles * GROUPS)
            if n >= 8:
                pe.wait_ge(rest, n - 7)
            src = pl.mixab if k < 4 else pl.mixc
            for t in range(tn // P):
                tr = pe.transpose(pl.bank(n % 8)[:, t * P:(t + 1) * P],
                                  src[:, t0 // P + t, (k % 4) * P:(k % 4 + 1) * P], pl.c(IDENT))
            tr.then_inc(turned, 1)

    def vector(dve, between=None):
        dve.wait_ge(rooted, 1)
        dve.reciprocal(rs[:, 1, 0:tiles, :], rs[:, 0, 0:tiles, :]).then_inc(inverted, 1)
        dve.wait_ge(inverted, 1)
        for t in range(tiles):
            for g in range(GROUPS):
                m = pl.mixc[:, t, 256 * g:256 * (g + 1)]
                dve.tensor_scalar(m, m, rs[:, 1, t, g:g + 1], None, ALU.mult).then_inc(normed, 1)
        for n, (k, c) in enumerate(items):
            t0, tn = CHUNKS[c]
            out, hi = pl.lo[:, k, t0:t0 + tn], raw(pl.hi[:, k, t0:t0 + tn])
            dve.wait_ge(rounded, n + 1)
            if k < 4:
                dve.tensor_tensor(out, pl.bank(n % 8, tn), hi, ALU.subtract).then_inc(rest, 1)
            else:
                dve.scalar_tensor_tensor(out=out, in0=pl.bank(n % 8, tn), scalar=gain(k), in1=hi,
                                         op0=ALU.mult, op1=ALU.subtract).then_inc(rest, 1)
        dve.wait_ge(x_in, 16)

    return Lead({c: [(rest, len(items))] for c in range(3)}, tensor, scalar, vector, sync=sync)



def project_out(pl, l, last, lead):
    nc, a = pl.nc, pl.a
    tag = f"o{l}"
    chunks = [c for c in ORDER if not (last and c == 2)]
    chunks_of = lambda kind: chunks
    segments = [(4, ["o", "o"])]
    ring = Ring(pl, tag, kb=170)
    full = [pl.sem(f"{tag}_full{c}") for c in range(3)]
    taken = [pl.sem(f"{tag}_taken{c}") for c in range(3)]
    ada = None if last else first_modulation(pl, l + 1)
    with nc.Block() as block:
        @block.scalar
        def _(act):
            lead.scalar(act)
            if ada is not None:
                ada.start(act)
                ada.silu(act)
                with act.Fori(0, G1 // ada.SLOTS) as r:
                    ada.load(act, r)

        @block.sync
        def _(sp):
            load = lambda at: ring.load(sp, at, a["w_out"][l, at.n])
            over(sp, [(1, ["o", "o"])], chunks_of, load)
            lead.sync(sp)
            over(sp, [(3, ["o", "o"])], chunks_of, load, start=2)

        @block.gpsimd
        def _(pool):
            pool.sem_inc(ring.ready, 2)
            over(pool, segments, chunks_of, lambda at: ring.split(pool, at, full[1]))

        @block.tensor
        def _(pe):
            pe.sem_inc(full[1], 2)
            lead.tensor(pe)
            pe.wait_ge(*lead.ready[1][0])
            over(pe, segments, chunks_of,
                 lambda at: multiply_block(pl, pe, ring, at, chunks, full, taken))

        @block.vector
        def _(dve):
            for c in range(3):
                dve.sem_inc(taken[c], 2)
            lead.vector(dve)
            if ada is not None:
                dve.wait_ge(ada.cond_ready, 1)

            def body(at):
                if ada is not None and at.j == 0:
                    ada.sums(dve, at.i)
                for c in chunks:
                    t0, tn = CHUNKS[c]
                    wait_full(dve, full, at, c)
                    who = 1 if c == 2 else 0
                    x = pl.x[:, at.n, t0:t0 + tn]
                    dve.scalar_tensor_tensor(out=x, in0=pl.bank(3 * at.par + c, tn),
                                             scalar=pl.mod[:, at.n + G1, who:who + 1], in1=x,
                                             op0=ALU.mult, op1=ALU.add).then_inc(taken[c], 1)
            over(dve, segments, chunks_of, body)
            if ada is not None:
                ada.finish(dve)



def normalise(pl, l, last, gcol, bcol, sc, sh, keep, place):
    tag = f"ln{l}{gcol}"
    final = keep == "out"
    chunks = (0, 1) if last else ORDER
    alpha = 1.0 if final else ALPHA
    pairs = KT // 2
    sd, ri = (pl.at(f"{tag}_{x}", [P, 512], F32, kb=b) for x, b in zip(("sd", "ri"), place))
    ga, ba = (pl.at(f"{tag}_{x}", [P, KT], F32, kb=b) for x, b in (("ga", 193), ("ba", 193.0625)))
    gm, bm = (pl.at(f"{tag}_{x}", [P, KT, 2], F32, kb=b) for x, b in (("gm", 193.125), ("bm", 193.25)))
    (factors, mean_full, centred, squared, sq_paired, var_full, rooted, inverted, normed, h_in, hi_in,
     split, x_done, stored) = (pl.sem(f"{tag}_{x}") for x in (
         "factors", "mean_full", "centred", "squared", "sq_paired", "var_full", "rooted",
         "inverted", "normed", "h_in", "hi_in", "split", "x_done", "stored"))
    N = len(chunks)
    late_split = pl.sem(f"{tag}_late_split")
    POOL_TILES = 5
    x_paired = [pl.sem(f"{tag}_x_paired{n}") for n in range(N)]

    def tile(n, k, t=None):
        t0, tn = CHUNKS[chunks[n]]
        return (pl.x if t is None else t)[:, k, t0:t0 + tn]

    def x_pair(n, j):
        return tile(n, j, pl.hi_f32)

    def sq_pair(n, j):
        return tile(n, pairs + j, pl.hi_f32)

    def who(n):
        return slice(1, 2) if chunks[n] == 2 else slice(0, 1)

    def pipeline(first, second):
        first(0)
        for n in range(N):
            if n + 1 < N:
                first(n + 1)
            second(n)

    def add_x_pairs(eng, n):
        for j in range(pairs):
            eng.tensor_tensor(x_pair(n, j), tile(n, 2 * j), tile(n, 2 * j + 1), ALU.add) \
                .then_inc(x_paired[n], 1)

    def tensor(pe):
        def mean(n):
            for j in range(pairs):
                pe.wait_ge(x_paired[n], j + 1)
                mm = pe.matmul(pl.bank(n, CHUNKS[chunks[n]][1]), pl.c(MEAN), x_pair(n, j),
                               start=(j == 0), stop=(j == pairs - 1))
            mm.then_inc(mean_full, 1)

        def variance(n):
            for j in range(pairs):
                pe.wait_ge(sq_paired, n * pairs + j + 1)
                mm = pe.matmul(pl.bank(4 + n, CHUNKS[chunks[n]][1]), pl.c(MEAN), sq_pair(n, j),
                               start=(j == 0), stop=(j == pairs - 1))
            mm.then_inc(var_full, 1)
        pipeline(mean, variance)
        pe.wait_ge(centred, N * KT)
        pe.wait_ge(rooted, N)

    def scalar(act):
        def square(n):
            for k in range(KT):
                act.wait_ge(centred, n * KT + k + 1)
                act.activation(tile(n, k, pl.lo_f32), tile(n, k), ACT.Square).then_inc(squared, 1)
            act.wait_ge(var_full, n + 1)
            if n >= 1:
                act.wait_ge(inverted, n)
            tn = CHUNKS[chunks[n]][1]
            act.activation(sd[:, 0:tn], pl.bank(4 + n, tn), ACT.Sqrt,
                           bias=pl.small[:, 1:2]).then_inc(rooted, 1)

        def scale(n):
            if n == 0:
                act.wait_ge(factors, 5)
            if not final:
                for k in range(KT):
                    act.wait_ge(normed, n * KT + k + 1)
                    act.activation(tile(n, k, pl.hi), tile(n, k), ACT.Identity,
                                   scale=gm[:, k, who(n)], bias=bm[:, k, who(n)]).then_inc(hi_in, 1)
            for k in range(KT):
                if final:
                    act.wait_ge(normed, n * KT + k + 1)
                else:
                    act.wait_ge(hi_in, n * KT + k + 1)
                    act.wait_ge(h_in, n * KT + k + 1)
                act.activation(tile(n, k), tile(n, k), ACT.Identity, scale=ga[:, k:k + 1],
                               bias=ba[:, k:k + 1]).then_inc(x_done, 1)
                if keep is not None and k % 4 == 3:
                    t0, tn = CHUNKS[chunks[n]]
                    act.wait_ge(x_done, n * KT + k + 1)
                    part = (slice(None), slice(k - 3, k + 1), slice(t0, t0 + tn))
                    dst = pl.a["out"] if final else pl.x_dram
                    act.dma_start(dst[part], pl.x[part]).then_inc(stored, 16)
        pipeline(square, scale)
        if keep is not None:
            act.wait_ge(stored, 16 * 2 * N)

    def vector(dve, between=None):
        g, b = pl.prm[:, gcol:gcol + KT], pl.prm[:, bcol:bcol + KT]
        for n in range(N - 1):
            add_x_pairs(dve, n)
        dve.tensor_scalar(ga[:, :], g, alpha, None, ALU.mult).then_inc(factors, 1)
        dve.tensor_scalar(ba[:, :], b, alpha, None, ALU.mult).then_inc(factors, 1)
        if not final:
            scales, shifts = pl.mod[:, sc:sc + KT, :], pl.mod[:, sh:sh + KT, :]
            wide = lambda v: v.unsqueeze(2).broadcast_to([P, KT, 2])
            dve.tensor_tensor(gm[:, :, :], scales, wide(g), ALU.mult).then_inc(factors, 1)
            dve.tensor_tensor(bm[:, :, :], scales, wide(b), ALU.mult).then_inc(factors, 1)
            dve.wait_ge(factors, 4)
            dve.tensor_tensor(bm[:, :, :], bm[:, :, :], shifts, ALU.add).then_inc(factors, 1)
            dve.wait_ge(factors, 5)
        else:
            dve.sem_inc(factors, 3)
        if between is not None:
            between()

        def centre(n):
            dve.wait_ge(mean_full, n + 1)
            for k in range(KT):
                dve.tensor_tensor(tile(n, k), tile(n, k), pl.bank(n, CHUNKS[chunks[n]][1]),
                                  ALU.subtract).then_inc(centred, 1)

        def norm(n):
            tn = CHUNKS[chunks[n]][1]
            dve.wait_ge(rooted, n + 1)
            if n >= 1:
                dve.wait_ge(normed, n * KT)
            dve.reciprocal(ri[:, 0:tn], sd[:, 0:tn]).then_inc(inverted, 1)
            dve.wait_ge(inverted, n + 1)

            def modulated(k):
                dve.wait_ge(normed, n * KT + k + 1)
                dve.tensor_scalar(tile(n, k, pl.lo_f32), tile(n, k), gm[:, k, who(n)], bm[:, k, who(n)],
                                  ALU.mult, ALU.add).then_inc(h_in, 1)
            for k in range(KT):
                dve.tensor_tensor(tile(n, k), tile(n, k), ri[:, 0:tn], ALU.mult).then_inc(normed, 1)
                if k and not final:
                    modulated(k - 1)
            if not final:
                modulated(KT - 1)
                if n == N - 1:
                    for k in range(POOL_TILES, KT):
                        dve.wait_ge(h_in, n * KT + k + 1)
                        dve.wait_ge(hi_in, n * KT + k + 1)
                        dve.tensor_tensor(tile(n, k, pl.lo), tile(n, k, pl.lo_f32),
                                          raw(tile(n, k, pl.hi)), ALU.subtract).then_inc(late_split, 1)
        pipeline(centre, norm)
        dve.wait_ge(x_done, N * KT)

    def gpsimd(pool):
        def add_sq_pairs(n):
            for j in range(pairs):
                pool.wait_ge(squared, n * KT + 2 * j + 2)
                pool.tensor_tensor(sq_pair(n, j), tile(n, 2 * j, pl.lo_f32),
                                   tile(n, 2 * j + 1, pl.lo_f32), ALU.add).then_inc(sq_paired, 1)

        def rest(n):
            for k in range(POOL_TILES if n == N - 1 else KT):
                if not final:
                    pool.wait_ge(h_in, n * KT + k + 1)
                    pool.wait_ge(hi_in, n * KT + k + 1)
                    pool.tensor_tensor(tile(n, k, pl.lo), tile(n, k, pl.lo_f32),
                                       raw(tile(n, k, pl.hi)), ALU.subtract).then_inc(split, 1)
        add_x_pairs(pool, N - 1)
        pipeline(add_sq_pairs, rest)

    ready = {c: [(split, (n + 1) * KT)] for n, c in enumerate(chunks)}
    ready[chunks[-1]] = [(split, (N - 1) * KT + POOL_TILES), (late_split, KT - POOL_TILES)]
    return Lead(ready, tensor, scalar, vector,
                gpsimd, prm_free=(factors, 5))


def run_alone(pl, lead):
    with pl.nc.Block() as block:
        @block.tensor
        def _(pe):
            lead.tensor(pe)

        @block.scalar
        def _(act):
            lead.scalar(act)

        @block.vector
        def _(dve):
            lead.vector(dve)

        @block.gpsimd
        def _(pool):
            lead.gpsimd(pool)



def feed_forward(pl, l, last, lead):
    nc, a = pl.nc, pl.a
    tag = f"f{l}"
    chunks = [c for c in ORDER if not (last and c == 2)]
    n_iter = FT // 2
    slot = [0, 1, 2, 0, 1, 2]
    n_down = KT * len(chunks)
    act_hi = pl.at(f"{tag}_ahi", [P, 2, TOK], F32R, kb=120)
    act_lo = pl.at(f"{tag}_alo", [P, 2, TOK], F32R, kb=130)
    gated = [pl.at(f"{tag}_gated{s}", [P, TOK], F32, kb=140 + 5 * s) for s in range(2)]
    wraw = [pl.at(f"{tag}_wraw{s}", [P, D], F32, kb=150 + 4 * s) for s in range(2)]
    w_hi = [pl.at(f"{tag}_whi{s}", [P, D], F32R, kb=158 + 4 * s) for s in range(3)]
    w_lo = [pl.at(f"{tag}_wlo{s}", [P, D], F32R, kb=170 + 4 * s) for s in range(3)]

    def sem(name):
        return pl.sem(f"{tag}_{name}")
    loaded = [sem(f"loaded{s}") for s in range(2)]
    rounded, ready = sem("rounded"), sem("ready")
    gu_full = {c: sem(f"gu_full{c}") for c in chunks}
    g_taken = {c: sem(f"g_taken{c}") for c in chunks}
    u_taken = {c: sem(f"u_taken{c}") for c in chunks}
    act_hi_in = {c: sem(f"act_hi_in{c}") for c in chunks}
    act_in = {c: sem(f"act_in{c}") for c in chunks}
    down_full, down_taken = sem("down_full"), sem("down_taken")

    with nc.Block() as block:
        @block.sync
        def _(sp):
            with sp.Fori(0, n_iter) as i:
                for j in range(6):
                    sp.wait_ge(ready, i * 6 + (j + 1))
                    sp.dma_start(wraw[j % 2][:, :], a["w_ffn"][l, i, j]).then_inc(loaded[j % 2], 16)

        @block.gpsimd
        def _(pool):
            pool.sem_inc(ready, 2)
            one = pl.small[:, 2:3].broadcast_to([P, D])

            def split(i, j):
                pool.wait_ge(loaded[j % 2], i * 48 + 16 * (j // 2 + 1))
                if j in (1, 2):
                    pool.wait_ge(down_full, i * n_down + 1)
                else:
                    pool.wait_ge(gu_full[1], i * 4 + {0: 1, 3: 2, 4: 3, 5: 4}[j])
                hi, lo = w_hi[slot[j]][:, :], w_lo[slot[j]][:, :]
                pool.tensor_tensor(hi, wraw[j % 2][:, :], one, ALU.mult).then_inc(rounded, 1)
                pool.wait_ge(rounded, i * 6 + (j + 1))
                pool.tensor_tensor(lo, wraw[j % 2][:, :], raw(hi), ALU.subtract).then_inc(ready, 1)

            def act_rest(i, f):
                for c in chunks:
                    t0, tn = CHUNKS[c]
                    pool.wait_ge(act_hi_in[c], i * 2 + (f + 1))
                    pool.tensor_tensor(act_lo[:, f, t0:t0 + tn], gated[f][:, t0:t0 + tn],
                                       raw(act_hi[:, f, t0:t0 + tn]), ALU.subtract).then_inc(act_in[c], 1)

            def iteration(i, first):
                for j in range(first, 4):
                    split(i, j)
                act_rest(i, 0)
                split(i, 4)
                split(i, 5)
                act_rest(i, 1)
            lead.gpsimd(pool)
            iteration(0, 2)
            with pool.Fori(1, n_iter) as i:
                iteration(i, 0)

        @block.tensor
        def _(pe):
            pe.sem_inc(gu_full[1], 1)
            pe.sem_inc(down_full, 1)
            lead.tensor(pe)
            with pe.Fori(0, n_iter) as i:
                for j in range(4):
                    f, up = j // 2, j % 2
                    hi = w_hi[slot[j]][:, :].rearrange("p (k n) -> p k n", n=P)
                    lo = w_lo[slot[j]][:, :].rearrange("p (k n) -> p k n", n=P)
                    pe.wait_ge(ready, i * 6 + (j + 3))
                    for c in chunks:
                        t0, tn = CHUNKS[c]
                        for sem, count in lead.ready[c]:
                            pe.wait_ge(sem, count)
                        pe.wait_ge((u_taken if up else g_taken)[c], i * 2 + (f + 1))
                        for k in range(KT):
                            mm = three_pass(pe, pl.bank(3 * up + c, tn), hi[:, k, :], lo[:, k, :],
                                            pl.hi[:, k, t0:t0 + tn], pl.lo[:, k, t0:t0 + tn],
                                            k == 0, k == KT - 1)
                        mm.then_inc(gu_full[c], 1)
                pe.wait_ge(ready, i * 6 + 8)
                d = 0
                for c in chunks:
                    t0, tn = CHUNKS[c]
                    pe.wait_ge(act_in[c], i * 2 + 2)
                    for n in range(KT):
                        pe.wait_ge(down_taken, i * n_down + (d + 1))
                        for f in range(2):
                            cols = slice(n * P, (n + 1) * P)
                            mm = three_pass(pe, pl.bank(6 + d % 2, tn), w_hi[1 + f][:, cols],
                                            w_lo[1 + f][:, cols], act_hi[:, f, t0:t0 + tn],
                                            act_lo[:, f, t0:t0 + tn], f == 0, f == 1)
                        mm.then_inc(down_full, 1)
                        d += 1

        @block.scalar
        def _(act):
            for c in chunks:
                act.sem_inc(g_taken[c], 1)
            for j in range(2):
                act.wait_ge(loaded[j], 16)
                act.activation(w_hi[j][:, :], wraw[j][:, :], ACT.Copy).then_inc(rounded, 1)
            lead.scalar(act)
            with act.Fori(0, n_iter) as i:
                for f in range(2):
                    for c in chunks:
                        t0, tn = CHUNKS[c]
                        act.wait_ge(gu_full[c], i * 4 + (2 * f + (2 if c == 1 else 1)))
                        act.activation(gated[f][:, t0:t0 + tn], pl.bank(c, tn), ACT.Silu) \
                            .then_inc(g_taken[c], 1)
                    for c in chunks:
                        t0, tn = CHUNKS[c]
                        act.wait_ge(u_taken[c], i * 2 + (f + 2))
                        act.activation(act_hi[:, f, t0:t0 + tn], gated[f][:, t0:t0 + tn], ACT.Copy) \
                            .then_inc(act_hi_in[c], 1)

        @block.vector
        def _(dve):
            for c in chunks:
                dve.sem_inc(u_taken[c], 1)
            dve.sem_inc(down_taken, 2)

            def rest_first():
                for j in range(2):
                    dve.wait_ge(rounded, j + 1)
                    dve.tensor_tensor(w_lo[j][:, :], wraw[j][:, :], raw(w_hi[j][:, :]),
                                      ALU.subtract).then_inc(ready, 1)
            lead.vector(dve, rest_first)
            with dve.Fori(0, n_iter) as i:
                for f in range(2):
                    for c in chunks:
                        t0, tn = CHUNKS[c]
                        dve.wait_ge(gu_full[c], i * 4 + (2 * f + (3 if c == 1 else 2)))
                        dve.wait_ge(g_taken[c], i * 2 + (f + 2))
                        g = gated[f][:, t0:t0 + tn]
                        dve.tensor_tensor(g, g, pl.bank(3 + c, tn), ALU.mult).then_inc(u_taken[c], 1)
                d = 0
                for c in chunks:
                    t0, tn = CHUNKS[c]
                    who = 1 if c == 2 else 0
                    for n in range(KT):
                        dve.wait_ge(down_full, i * n_down + (d + 2))
                        x = pl.x[:, n, t0:t0 + tn]
                        dve.scalar_tensor_tensor(out=x, in0=pl.bank(6 + d % 2, tn),
                                                 scalar=pl.mod[:, G2 + n, who:who + 1], in1=x,
                                                 op0=ALU.mult, op1=ALU.add).then_inc(down_taken, 1)
                        d += 1


def build(nc, arrays, stop=None):
    with ExitStack() as ctx:
        pl = Plan(nc, ctx, arrays)
        pl.xb = pl.at("xb_tok", [P, TT, 768], F32, kb=80)
        pl.bt = pl.at("b_feat", [P, GROUPS, TOK], F32, kb=110)
        pl.ct = pl.at("c_feat", [P, GROUPS, TOK], F32, kb=140)
        load_inputs(pl)
        pl.end_stage()
        before_ffn, before_ab = (120, 122), (164, 191)

        def lead_in(l):
            if l == 0:
                return modulate_inputs(pl)
            return normalise(pl, l - 1, False, LN2G, LN2B, SC1, SH1, "dram", before_ab)
        for l in range(DEPTH):
            last = l == DEPTH - 1
            stages = [
                ("ab", lambda: project_attention(pl, l, last, lead_in(l))),
                ("rope", lambda: norm_and_rotate(pl, l, last)),
                ("attn", lambda: attend(pl, l, last)),
                ("c", lambda: project_ssd(pl, l, last)),
                ("ssd", lambda: scan(pl, l, last)),
                ("out", lambda: project_out(pl, l, last, gather_mix(pl, l, last))),
                ("ffn", lambda: feed_forward(pl, l, last, normalise(
                    pl, l, last, LN1G, LN1B, SC2, SH2, None, before_ffn))),
            ]
            for name, stage in stages:
                stage()
                pl.end_stage()
                if stop == (l, name):
                    return pl
        run_alone(pl, normalise(pl, DEPTH - 1, True, LN2G, LN2B, None, None, "out", before_ffn))
        pl.end_stage()
    return pl



def lay_out(x, c, ctx, c_ctx, w_ada, b_ada, w_in, sink, q_gain, k_gain, conv_w, conv_b, a_log, dt_bias,
            d_skip, gnorm_w, w_out, ln1_g, ln1_b, ln2_g, ln2_b, w_gu, w_down):
    f = np.ascontiguousarray

    def feature_major(t):
        return t.T.reshape(KT, P, t.shape[0]).transpose(1, 0, 2)

    def columns(v):
        return v.reshape(DEPTH, -1, P).transpose(0, 2, 1)

    def rows(v):
        return np.broadcast_to(v.reshape(DEPTH, 1, -1), (DEPTH, P, v.size // DEPTH))

    def blocks(w, n):
        return w.reshape(DEPTH, w.shape[1] // P, P, -1, n).transpose(0, 3, 2, 1, 4)

    order = []
    for base in (0, 512):
        for heads in ((0, 2), (1, 3)):
            for h in heads:
                order += list(range(base + HD * h, base + HD * (h + 1)))
        order += list(range(base + 256, base + 512))
    order += list(range(1024, 2560)) + list(range(2576 - P, 2576))
    w_gate, w_up = blocks(w_gu[:, :, :D_FF], P), blocks(w_gu[:, :, D_FF:], P)
    down = w_down.reshape(DEPTH, FT, P, KT, P)
    w_ffn = np.stack([w_gate[:, 0::2], w_up[:, 0::2], w_gate[:, 1::2], w_up[:, 1::2],
                      down[:, 0::2], down[:, 1::2]], 2)
    conv = conv_w.transpose(0, 2, 1).reshape(DEPTH, 8, P, CONV).transpose(0, 2, 1, 3)
    gain = lambda g: np.concatenate([g, g], 1)[:, :, None]
    prm = np.concatenate([columns(ln1_g), columns(ln1_b), columns(ln2_g), columns(ln2_b),
                          conv.reshape(DEPTH, P, 8 * CONV), columns(conv_b), gain(q_gain), gain(k_gain),
                          rows(sink), rows(dt_bias), rows(a_log), rows(d_skip), columns(gnorm_w)], 2)
    xT = np.concatenate([feature_major(x[0]), feature_major(ctx[0])], 2)
    return {
        "consts": const_table(), "rope": rope_table(), "xT": f(xT), "prm": f(prm),
        "cond": f(np.broadcast_to(np.stack([c[0], c_ctx]), (P, 2, D))), "b_ada": f(columns(b_ada)),
        "w_ada": f(w_ada.transpose(0, 2, 1).reshape(DEPTH, 48, P, D)),
        "w_in": f(blocks(w_in[:, :, order], P).reshape(DEPTH, 21, P, D)),
        "w_out": f(blocks(w_out, P).reshape(DEPTH, KT, P, D)),
        "w_ffn": f(w_ffn.reshape(DEPTH, FT // 2, 6, P, D)),
    }


def kernel(**inputs):
    import concourse.bacc as bacc
    from concourse.bass_utils import run_bass_kernel_spmd

    nc = bacc.Bacc("TRN2", target_bir_lowering=False, num_devices=1)
    data = lay_out(**{k: np.asarray(v) for k, v in inputs.items()})
    arrays = {k: nc.dram_tensor(f"in_{k}", v.shape, F32, kind="ExternalInput").ap() for k, v in data.items()}
    arrays["out"] = nc.dram_tensor("out_x", (P, KT, SEQ), F32, kind="ExternalOutput").ap()
    build(nc, arrays)
    r = run_bass_kernel_spmd(nc, [{f"in_{k}": v for k, v in data.items()}], core_ids=[0])
    y = r.results[0]["out_x"]
    return np.ascontiguousarray(y.transpose(1, 0, 2).reshape(D, SEQ).T)[None]
```
